# Optimizing a Trainium2 kernel written in Bass

```python
import jax
import jax.numpy as jnp
from jax import lax
import numpy as np

D_MODEL = 1024
BATCH = 1
SEQ = 256
DEPTH = 2

GRID_W = 64
CTX_LEN = 256

RET_HEADS = 4
RET_DK = 128
RET_DV = 256
RET_CHUNK = 128
RET_GAMMA_EXP0 = 5

NA_HEADS = 8
NA_DH = 64
NA_KH_MAX = 8
NA_KW = 16

FOU_GROUPS = 4
FOU_DG = 128

N_BRANCH = 3
D_FF = 2816
ROPE_BASE = 10000.0
LN_EPS = 1e-6

RET_QK_W = RET_HEADS * RET_DK
RET_V_W = RET_HEADS * RET_DV
NA_W = NA_HEADS * NA_DH
FOU_W = FOU_GROUPS * FOU_DG
SPLIT_SIZES = (RET_QK_W, RET_QK_W, RET_V_W, RET_V_W, NA_W, NA_W, NA_W, FOU_W, N_BRANCH * D_MODEL)
SPLIT_POINTS = tuple(sum(SPLIT_SIZES[:i + 1]) for i in range(len(SPLIT_SIZES) - 1))
D_IN = sum(SPLIT_SIZES)
DEEPNORM_ALPHA = (2 * DEPTH) ** 0.25
DEEPNORM_BETA = (8 * DEPTH) ** -0.25

kernel_name = 'hybrid_retention_natten_fnet_prefix_trunk'

def layer_norm(x, w=None, b=None):
    xf = x.astype(jnp.float32)
    mu = xf.mean(-1, keepdims=True)
    var = jnp.square(xf - mu).mean(-1, keepdims=True)
    y = (xf - mu) * lax.rsqrt(var + LN_EPS)
    if w is not None:
        y = y * w.astype(jnp.float32) + b.astype(jnp.float32)
    return y.astype(x.dtype)

def modulate(x, shift, scale):
    return layer_norm(x) * (1.0 + scale) + shift

def swiglu(h, w1, w3, w2):
    return (jax.nn.silu(h @ w1) * (h @ w3)) @ w2

def ffn_sublayer(s, mods, w1, w3, w2, lw, lb):
    shift, scale, gate = mods
    h = modulate(s, shift, scale)
    return layer_norm(DEEPNORM_ALPHA * s + 0.5 * gate * swiglu(h, w1, w3, w2), lw, lb)

def to_heads(t, n_heads, d):
    b, n, _ = t.shape
    return t.reshape(b, n, n_heads, d).transpose(0, 2, 1, 3)

def axial_rope(x, row, col):
    def rot(xa, pos):
        half = xa.shape[-1] // 2
        freqs = ROPE_BASE ** (-jnp.arange(half, dtype=jnp.float32) / half)
        ang = pos.astype(jnp.float32)[:, None] * freqs[None, :]
        cos = jnp.cos(ang).astype(xa.dtype)
        sin = jnp.sin(ang).astype(xa.dtype)
        x1, x2 = xa[..., :half], xa[..., half:]
        return jnp.concatenate([x1 * cos - x2 * sin, x1 * sin + x2 * cos], axis=-1)
    h = x.shape[-1] // 2
    return jnp.concatenate([rot(x[..., :h], row), rot(x[..., h:], col)], axis=-1)

def retention_scan(q, k, v, log_g, s0, include_diag):
    b, h, n, dk = q.shape
    dv = v.shape[-1]
    nc = n // RET_CHUNK
    idx = jnp.arange(RET_CHUNK, dtype=jnp.float32)
    diff = idx[:, None] - idx[None, :]
    mask = diff >= 0 if include_diag else diff > 0
    dmat = jnp.where(mask[None], jnp.exp(log_g[:, None, None] * jnp.maximum(diff, 0.0)[None]), 0.0)
    q_decay = jnp.exp(log_g[:, None] * (idx + 1.0)[None, :])
    k_decay = jnp.exp(log_g[:, None] * (RET_CHUNK - 1.0 - idx)[None, :])
    chunk_decay = jnp.exp(log_g * RET_CHUNK)

    def chunks(t):
        return t.reshape(b, h, nc, RET_CHUNK, t.shape[-1]).transpose(2, 0, 1, 3, 4)

    def step(s, inp):
        qi, ki, vi = inp
        inner = jnp.einsum('bhid,bhjd->bhij', qi, ki) * dmat
        o = jnp.einsum('bhij,bhjv->bhiv', inner, vi) + jnp.einsum('bhid,bhdv->bhiv', qi, s) * q_decay[:, :, None]
        s = s * chunk_decay[:, None, None] + jnp.einsum('bhjd,bhjv->bhdv', ki * k_decay[:, :, None], vi)
        return s, o

    _, o = lax.scan(step, s0, (chunks(q), chunks(k), chunks(v)))
    return o.transpose(1, 2, 0, 3, 4).reshape(b, h, n, dv)

def retention_final_state(k, v, log_g, reverse):
    n = k.shape[2]
    m = jnp.arange(n, dtype=jnp.float32)
    e = m if reverse else (n - 1.0 - m)
    w = jnp.exp(log_g[:, None] * e[None, :])
    return jnp.einsum('bhmd,bhmv->bhdv', k * w[None, :, :, None], v)

def bidir_retention(q, k, v, log_g, s_fwd, s_bwd):
    flip = lambda a: jnp.flip(a, axis=2)
    fwd = retention_scan(q, k, v, log_g[0], s_fwd, True)
    bwd = flip(retention_scan(flip(q), flip(k), flip(v), log_g[1], s_bwd, False))
    return fwd + bwd

def retention_out(o, g, gn_w, gn_b, w_out):
    mu = o.mean(-1, keepdims=True)
    var = jnp.square(o - mu).mean(-1, keepdims=True)
    o = (o - mu) * lax.rsqrt(var + LN_EPS)
    b, h, n, dv = o.shape
    o = o.transpose(0, 2, 1, 3).reshape(b, n, h * dv) * gn_w.astype(jnp.float32) + gn_b.astype(jnp.float32)
    return (o.astype(g.dtype) * jax.nn.silu(g)) @ w_out

def neighbourhood_attention(q, k, v, kc, vc, rpb, rows):
    kh = min(NA_KH_MAX, rows)
    scale = NA_DH ** -0.5
    cols = jnp.arange(GRID_W)
    col_start = jnp.clip(cols - NA_KW // 2, 0, GRID_W - NA_KW)
    col_idx = col_start[:, None] + jnp.arange(NA_KW)[None, :]
    dc = col_idx - cols[:, None] + NA_KW - 1
    rpb_c = rpb[:, :, dc]

    def row_fn(r):
        r0 = jnp.clip(r - kh // 2, 0, rows - kh)
        qr = lax.dynamic_index_in_dim(q, r, axis=2, keepdims=False)
        kb = lax.dynamic_slice_in_dim(k, r0, kh, axis=2)
        vb = lax.dynamic_slice_in_dim(v, r0, kh, axis=2)
        kn = kb[:, :, :, col_idx]
        vn = vb[:, :, :, col_idx]
        dr = r0 + jnp.arange(kh) - r + NA_KH_MAX - 1
        bias = jnp.transpose(rpb_c[:, dr], (0, 2, 1, 3))
        s_loc = jnp.einsum('bhqd,bhiqjd->bhqij', qr, kn) * scale + bias
        s_ctx = jnp.einsum('bhqd,bhmd->bhqm', qr, kc) * scale
        bsz, hh, wq = s_loc.shape[:3]
        s = jnp.concatenate([s_loc.reshape(bsz, hh, wq, kh * NA_KW), s_ctx], axis=-1).astype(jnp.float32)
        p = jax.nn.softmax(s, axis=-1).astype(v.dtype)
        p_loc = p[..., :kh * NA_KW].reshape(bsz, hh, wq, kh, NA_KW)
        p_ctx = p[..., kh * NA_KW:]
        return jnp.einsum('bhqij,bhiqjd->bhqd', p_loc, vn) + jnp.einsum('bhqm,bhmd->bhqd', p_ctx, vc)

    return lax.map(row_fn, jnp.arange(rows))

def context_attention(q, k, v):
    s = (jnp.einsum('bhnd,bhmd->bhnm', q, k) * NA_DH ** -0.5).astype(jnp.float32)
    p = jax.nn.softmax(s, axis=-1).astype(v.dtype)
    return jnp.einsum('bhnm,bhmd->bhnd', p, v)

def fourier_mix(u):
    b, n, _ = u.shape
    ug = u.reshape(b, n, FOU_GROUPS, FOU_DG).astype(jnp.float32)
    f = jnp.fft.fft2(ug, axes=(1, 3), norm='ortho').real
    return f.reshape(b, n, FOU_W).astype(u.dtype)

def token_mixer(hx, hc, w_in, ret_decay_logit, ret_gn_w, ret_gn_b, ret_w_out, na_rpb, na_w_out,
                fou_w_out, w_o, ctx_out):
    b, n_lat, _ = hx.shape
    rows = n_lat // GRID_W
    rq_x, rk_x, rv_x, rg_x, nq_x, nk_x, nv_x, fu_x, gt_x = jnp.split(hx @ w_in, SPLIT_POINTS, axis=-1)
    rq_c, rk_c, rv_c, rg_c, nq_c, nk_c, nv_c, fu_c, gt_c = jnp.split(hc @ w_in, SPLIT_POINTS, axis=-1)
    log_g = jax.nn.log_sigmoid(ret_decay_logit.astype(jnp.float32))
    f32 = jnp.float32

    t = jnp.arange(n_lat)
    row, col = t // GRID_W, t % GRID_W
    q_x = axial_rope(to_heads(rq_x, RET_HEADS, RET_DK).astype(f32) * RET_DK ** -0.5, row, col)
    k_x = axial_rope(to_heads(rk_x, RET_HEADS, RET_DK).astype(f32), row, col)
    v_x = to_heads(rv_x, RET_HEADS, RET_DV).astype(f32)
    k_c = to_heads(rk_c, RET_HEADS, RET_DK).astype(f32)
    v_c = to_heads(rv_c, RET_HEADS, RET_DV).astype(f32)
    s_fwd = retention_final_state(k_c, v_c, log_g[0], False)
    s_bwd = retention_final_state(k_c, v_c, log_g[1], True)
    y_ret = retention_out(bidir_retention(q_x, k_x, v_x, log_g, s_fwd, s_bwd), rg_x, ret_gn_w, ret_gn_b, ret_w_out)

    def grid_heads(a):
        return a.reshape(b, rows, GRID_W, NA_HEADS, NA_DH).transpose(0, 3, 1, 2, 4)
    kc_na = to_heads(nk_c, NA_HEADS, NA_DH)
    vc_na = to_heads(nv_c, NA_HEADS, NA_DH)
    o_na = neighbourhood_attention(grid_heads(nq_x), grid_heads(nk_x), grid_heads(nv_x), kc_na, vc_na, na_rpb, rows)
    y_na = o_na.transpose(1, 0, 3, 2, 4).reshape(b, n_lat, NA_W) @ na_w_out

    y_fou = fourier_mix(fu_x) @ fou_w_out

    g_ret, g_na, g_fou = jnp.split(gt_x, N_BRANCH, axis=-1)
    y_x = (jax.nn.sigmoid(g_ret) * y_ret + jax.nn.sigmoid(g_na) * y_na + jax.nn.sigmoid(g_fou) * y_fou) @ w_o
    if not ctx_out:
        return y_x, None

    n_ctx = hc.shape[1]
    q_c = to_heads(rq_c, RET_HEADS, RET_DK).astype(f32) * RET_DK ** -0.5
    zeros = jnp.zeros((b, RET_HEADS, RET_DK, RET_DV), f32)
    yc_ret = retention_out(bidir_retention(q_c, k_c, v_c, log_g, zeros, zeros), rg_c, ret_gn_w, ret_gn_b, ret_w_out)
    o_cna = context_attention(to_heads(nq_c, NA_HEADS, NA_DH), kc_na, vc_na)
    yc_na = o_cna.transpose(0, 2, 1, 3).reshape(b, n_ctx, NA_W) @ na_w_out
    yc_fou = fourier_mix(fu_c) @ fou_w_out
    gc_ret, gc_na, gc_fou = jnp.split(gt_c, N_BRANCH, axis=-1)
    y_c = (jax.nn.sigmoid(gc_ret) * yc_ret + jax.nn.sigmoid(gc_na) * yc_na + jax.nn.sigmoid(gc_fou) * yc_fou) @ w_o
    return y_x, y_c

def setup_inputs(seed: int = 0) -> dict:
    key = jax.random.key(seed)
    ks = jax.random.split(key, 26)
    f32 = jnp.float32
    beta = DEEPNORM_BETA

    def nrm(k, shape, scale):
        return jax.random.normal(k, shape, f32) * scale

    col_scales = (1.0, 1.0, beta, 1.0, 1.0, 1.0, beta, beta, 1.0)
    col_scale = jnp.concatenate([jnp.full((s,), v, f32) for s, v in zip(SPLIT_SIZES, col_scales)])
    gamma0 = 1.0 - 2.0 ** (-(RET_GAMMA_EXP0 + np.arange(RET_HEADS)))
    logit0 = jnp.asarray(np.log(gamma0 / (1.0 - gamma0)), f32)
    return {
        'x': nrm(ks[0], (BATCH, SEQ, D_MODEL), 1.0),
        'c': nrm(ks[1], (BATCH, D_MODEL), 1.0),
        'ctx': nrm(ks[2], (BATCH, CTX_LEN, D_MODEL), 1.0),
        'c_ctx': nrm(ks[3], (D_MODEL,), 1.0),
        'ada_w': nrm(ks[4], (DEPTH, D_MODEL, 9 * D_MODEL), 0.5 * D_MODEL ** -0.5),
        'ada_b': nrm(ks[5], (DEPTH, 9 * D_MODEL), 0.02),
        'ln_w': 1.0 + nrm(ks[6], (DEPTH, 3, D_MODEL), 0.02),
        'ln_b': nrm(ks[7], (DEPTH, 3, D_MODEL), 0.02),
        'ffa_w1': nrm(ks[8], (DEPTH, D_MODEL, D_FF), D_MODEL ** -0.5),
        'ffa_w3': nrm(ks[9], (DEPTH, D_MODEL, D_FF), D_MODEL ** -0.5),
        'ffa_w2': nrm(ks[10], (DEPTH, D_FF, D_MODEL), beta * D_FF ** -0.5),
        'mix_w_in': nrm(ks[11], (DEPTH, D_MODEL, D_IN), D_MODEL ** -0.5) * col_scale,
        'ret_decay_logit': logit0[None, None, :] + nrm(ks[12], (DEPTH, 2, RET_HEADS), 0.1),
        'ret_gn_w': 1.0 + nrm(ks[13], (DEPTH, RET_V_W), 0.02),
        'ret_gn_b': nrm(ks[14], (DEPTH, RET_V_W), 0.02),
        'ret_w_out': nrm(ks[15], (DEPTH, RET_V_W, D_MODEL), beta * RET_V_W ** -0.5),
        'na_rpb': nrm(ks[16], (DEPTH, NA_HEADS, 2 * NA_KH_MAX - 1, 2 * NA_KW - 1), 0.1),
        'na_w_out': nrm(ks[17], (DEPTH, NA_W, D_MODEL), beta * NA_W ** -0.5),
        'fou_w_out': nrm(ks[18], (DEPTH, FOU_W, D_MODEL), beta * FOU_W ** -0.5),
        'mix_w_o': nrm(ks[19], (DEPTH, D_MODEL, D_MODEL), beta * D_MODEL ** -0.5),
        'ffb_w1': nrm(ks[20], (DEPTH, D_MODEL, D_FF), D_MODEL ** -0.5),
        'ffb_w3': nrm(ks[21], (DEPTH, D_MODEL, D_FF), D_MODEL ** -0.5),
        'ffb_w2': nrm(ks[22], (DEPTH, D_FF, D_MODEL), beta * D_FF ** -0.5),
    }

def reference(x, c, ctx, c_ctx, ada_w, ada_b, ln_w, ln_b, ffa_w1, ffa_w3, ffa_w2, mix_w_in,
              ret_decay_logit, ret_gn_w, ret_gn_b, ret_w_out, na_rpb, na_w_out, fou_w_out, mix_w_o,
              ffb_w1, ffb_w3, ffb_w2):
    for l in range(DEPTH):
        last = l == DEPTH - 1
        mods_x = jnp.split((jax.nn.silu(c) @ ada_w[l] + ada_b[l])[:, None, :], 9, axis=-1)
        mods_c = jnp.split((jax.nn.silu(c_ctx) @ ada_w[l] + ada_b[l])[None, None, :], 9, axis=-1)

        x = ffn_sublayer(x, mods_x[0:3], ffa_w1[l], ffa_w3[l], ffa_w2[l], ln_w[l, 0], ln_b[l, 0])
        ctx = ffn_sublayer(ctx, mods_c[0:3], ffa_w1[l], ffa_w3[l], ffa_w2[l], ln_w[l, 0], ln_b[l, 0])

        sh_x, sc_x, g_x = mods_x[3:6]
        sh_c, sc_c, g_c = mods_c[3:6]
        y_x, y_c = token_mixer(modulate(x, sh_x, sc_x), modulate(ctx, sh_c, sc_c), mix_w_in[l],
                               ret_decay_logit[l], ret_gn_w[l], ret_gn_b[l], ret_w_out[l], na_rpb[l],
                               na_w_out[l], fou_w_out[l], mix_w_o[l], not last)
        x = layer_norm(DEEPNORM_ALPHA * x + g_x * y_x, ln_w[l, 1], ln_b[l, 1])

        x = ffn_sublayer(x, mods_x[6:9], ffb_w1[l], ffb_w3[l], ffb_w2[l], ln_w[l, 2], ln_b[l, 2])
        if not last:
            ctx = layer_norm(DEEPNORM_ALPHA * ctx + g_c * y_c, ln_w[l, 1], ln_b[l, 1])
            ctx = ffn_sublayer(ctx, mods_c[6:9], ffb_w1[l], ffb_w3[l], ffb_w2[l], ln_w[l, 2], ln_b[l, 2])
    return x


_drawn_inputs = setup_inputs


def setup_inputs(seed=0):
    import zlib

    import numpy as np

    out = dict(_drawn_inputs(seed))
    spreads = {}
    factors = {'ctx': 5.552,
     'c_ctx': 4.873,
     'ada_b': 8.0,
     'ret_decay_logit': 35.616,
     'ret_gn_w': 64.0,
     'ret_gn_b': 64.0,
     'na_rpb': 29.35,
     'na_w_out': 8.0,
     'fou_w_out': 3.363}
    for name, (base, spread) in spreads.items():
        noise = np.random.default_rng([zlib.crc32(name.encode()), seed]).standard_normal(out[name].shape)
        drawn = base * np.exp(spread * noise) if base else spread * noise
        out[name] = jnp.asarray(drawn.astype(out[name].dtype))
    for name, factor in factors.items():
        out[name] = (out[name] * factor).astype(out[name].dtype)
    return out
```

```python
from contextlib import ExitStack

import concourse.bass as bass
from concourse import mybir

F32 = mybir.dt.float32
F32R = mybir.dt.float32r
ALU = mybir.AluOpType
ACT = mybir.ActivationFunctionType
AXX = mybir.AxisListType.X

P = 128
D = 1024
KD = D // P
SEQ = CTX = 256
TOK = SEQ + CTX
NT = TOK // P
LT = SEQ // P
DEPTH = 2
FF = 2816
KF = FF // P
GRID_W = 64
ROWS = SEQ // GRID_W
RH, DK, DV = 4, 128, 256
NH, DH = 8, 64
FG = 4
RPB_R, RPB_C = 15, 31
TAB = 128
EPS = 1e-6
ALPHA = float((2 * DEPTH) ** 0.25)

C_RQ, C_RK, C_RV, C_RG = 0, 512, 1024, 2048
C_NQ, C_NK, C_NV, C_FU, C_GT = 3072, 3584, 4096, 4608, 5120

RING = 4
UN = 1024
ADA_G = 6
ADA_U = 4
ADA_IT = 6
FFN_IT = KF // 2
SUBS = 3 * DEPTH

N_FFN_ADA = FFN_IT * 4 + ADA_IT * 4
N_FFN = FFN_IT * 4


def plan():
    at, u = {}, 0

    def put(name, n):
        nonlocal u
        at[name] = u
        u += n

    put("ada", ADA_G * ADA_U)
    for l in range(DEPTH):
        put(("w13", 3 * l), N_FFN_ADA)
        put(("w2", 3 * l), KF)
        put(("ret_in", l), 4 * 8)
        put(("rv", l), 8)
        put(("fu", l), 4)
        put(("na_in", l), 2 * 8)
        put(("nv", l), 4)
        put(("merge", l), 8 * 5)
        put(("wo", l), 8)
        put(("w13", 3 * l + 2), N_FFN_ADA if l < DEPTH - 1 else N_FFN)
        put(("w2", 3 * l + 2), KF)
    at["end"] = u
    return at


def trunk(nc, io, out):
    AT = plan()
    END = AT["end"]
    ctx = ExitStack()
    with ctx:
        def sem(name):
            return ctx.enter_context(nc.semaphore(name))

        def sb(name, shape, dt=F32, scope=ctx):
            return scope.enter_context(nc.sbuf_tensor(name, shape, dt))

        ps = ctx.enter_context(nc.psum_tensor("ps", [P, 8, 512], F32))

        x = sb("x_res", [P, NT, D])
        raw = sb("raw", [P, RING, UN])
        wh = sb("wh", [P, RING, UN], F32R)
        wl = sb("wl", [P, RING, UN], F32R)
        hh = sb("hh", [P, KD, TOK], F32R)
        hl = sb("hl", [P, KD, TOK], F32R)
        sh_ = sb("stage_h", [P, 2, TOK], F32R)
        sl_ = sb("stage_l", [P, 2, TOK], F32R)
        cs = sb("cs", [P, KD, P], F32R)
        mod4 = sb("mod4", [4, 3 * D])
        grow = sb("grow", [4, D])
        modT = sb("modT", [P, 2, KD, 2])
        ident = sb("ident", [P, P])
        flip = sb("flip", [P, P])
        swap = sb("swap", [P, P])
        ropeC = sb("ropeC", [P, SEQ])
        ropeS = sb("ropeS", [P, SEQ])
        dft_d = sb("dft_d", [P, 2 * P])
        dft_n = sb("dft_n", [P, 2, 2, SEQ])
        wmask = sb("wmask", [P, GRID_W])
        mean256 = sb("mean256", [P, P])
        sel = sb("sel", [4, 2])
        selb = sb("selb", [4, 2, P])
        gnw = sb("gnw", [P, DEPTH, KD])
        gnb = sb("gnb", [P, DEPTH, KD])
        lgt = sb("lgt", [P, DEPTH * 2 * RH])
        small = sb("small", [P, 8, DEPTH * 2 * RH])
        c2 = sb("c2", [P, 2, KD])
        c2s = sb("c2s", [P, 2, KD])
        st = sb("st", [P, 2, NT, 12])
        mv = sb("mv", [P, 2, NT, 4])
        nhalf = sb("nhalf", [P, LT])
        rve = sb("rve", [P, 2, LT])
        nmax = sb("nmax", [P, 2, 4])

        def transition(scope):
            return (sb("lnw" + scope.tag, [P, D], scope=scope), sb("lnb" + scope.tag, [P, D], scope=scope),
                    sb("gateB" + scope.tag, [P, 2, D], scope=scope),
                    sb("tA" + scope.tag, [P, 2, D], scope=scope), sb("tB" + scope.tag, [P, NT, D], scope=scope))

        class Scope(ExitStack):
            tag = ""

        with Scope() as ffn:
            ffn.tag = "_f"
            g = sb("g", [P, KF, TOK], scope=ffn)
            T_ffn = transition(ffn)
            pad = T_ffn[4][0:NH * RPB_R, 2, 0:DEPTH * TAB].rearrange("p (l c) -> p l c", l=DEPTH)
        with Scope() as mix:
            rgz = sb("rgz", [P, KD, TOK], scope=mix)
            with Scope() as s:
                s.tag = "_m"
                T_mix = transition(s)
            with Scope() as s:
                kq = sb("kq", [P, 8, TOK], scope=s)
                rv = sb("rv", [P, NT, RH * DV], scope=s)
                dist = sb("dist", [P, 4, 2, SEQ], scope=s)
                dec = sb("dec", [P, 2, 4, SEQ], scope=s)
                dec2 = sb("dec2", [P, 2, SEQ], scope=s)
                rp = sb("rp", [P, 2, 4, SEQ], scope=s)
                ro = sb("ro", [P, 2, 2, SEQ], scope=s)
                rq2 = sb("rq2", [P, 2, SEQ], scope=s)
                rr = sb("rr", [P, 2, LT, P], scope=s)
            fh = sb("fh", [P, FG, TOK], F32R, scope=mix)
            fl = sb("fl", [P, FG, TOK], F32R, scope=mix)
            ah = sb("ah", [P, FG, TOK], F32R, scope=mix)
            al = sb("al", [P, FG, TOK], F32R, scope=mix)
            with Scope() as s:
                fu = sb("fu", [P, FG, TOK], scope=s)
                fA = sb("fA", [P, 2, 2, 2 * P], scope=s)
            with Scope() as s:
                nkq = sb("nkq", [P, 2, 4, TOK], scope=s)
                nv = sb("nv", [P, NT, NH * DH], scope=s)
                bias = sb("bias", [P, 2, LT, SEQ], scope=s)
                prob = sb("prob", [P, 2, TOK], scope=s)
                probT = sb("probT", [P, 2, TOK], scope=s)
                jd = sb("jd", [P, 2, P], scope=s)
            with Scope() as s:
                oh = sb("oh", [P, KD, TOK], F32R, scope=s)
                ol = sb("ol", [P, KD, TOK], F32R, scope=s)
                sg = sb("sg", [P, 3, TOK], scope=s)
        tab = nc.dram_tensor("rpb_table", [DEPTH, NH, RPB_R, TAB], F32).ap()

        loaded = [sem(f"loaded{i}") for i in range(RING)]
        w_rounded, w_split, unit_done = sem("w_rounded"), sem("w_split"), sem("unit_done")
        const_in, pad_zero, pad_in, tab_in, dist_in = [sem(n) for n in ("const_in", "pad_zero", "pad_in", "tab_in", "dist_in")]
        x_in, tables_set, c_sig, c_silu, c_hi, c_lo = [sem(n) for n in ("x_in", "tables_set", "c_sig", "c_silu", "c_hi", "c_lo")]
        lg_abs, lg_exp, lg_ready = sem("lg_abs"), sem("lg_exp"), sem("lg_ready")
        mod_zero, mod_bias, ada_sum = sem("mod_zero"), sem("mod_bias"), sem("ada_sum")
        gate_mm, gate_ready, mods_mm, mods_ready = [sem(n) for n in ("gate_mm", "gate_ready", "mods_mm", "mods_ready")]
        ln_in, post_stat, post_rstd, x_ready = [sem(n) for n in ("ln_in", "post_stat", "post_rstd", "x_ready")]
        pre_stat, pre_rstd, pre_norm, h_turned, h_mod, h_hi, h_lo = [
            sem(n) for n in ("pre_stat", "pre_rstd", "pre_norm", "h_turned", "h_mod", "h_hi", "h_lo")]
        ff_sig, ff_gate, ff_mul = sem("ff_sig"), sem("ff_gate"), sem("ff_mul")
        stage_hi, stage_lo = sem("stage_hi"), sem("stage_lo")
        in_copied, rv_copied, nv_copied = sem("in_copied"), sem("rv_copied"), sem("nv_copied")
        rg_sig, rg_silu = sem("rg_sig"), sem("rg_silu")
        rope_mm, rope_done = sem("rope_mm"), sem("rope_done")
        dec_arg, dec_exp, dec_ready = sem("dec_arg"), sem("dec_exp"), sem("dec_ready")
        r_score, r_prob, r_out, r_copied, r_mean, r_cent, r_sq, r_var, r_vare, r_rstd, r_diag, r_spread, r_fin = [
            sem(n) for n in ("r_score", "r_prob", "r_out", "r_copied", "r_mean", "r_cent", "r_sq", "r_var", "r_vare", "r_rstd", "r_diag", "r_spread", "r_fin")]
        f_one, f_onec, f_two, f_hi, f_lo = [sem(n) for n in ("f_one", "f_onec", "f_two", "f_hi", "f_lo")]
        bias_in = [sem(f"bias_in{i}") for i in range(2)]
        bias_masked = sem("bias_masked")
        n_score, n_max, n_exp, n_jd, n_turn, n_turnc, n_out, n_hi, n_lo = [
            sem(n) for n in ("n_score", "n_max", "n_exp", "n_jd", "n_turn", "n_turnc", "n_out", "n_hi", "n_lo")]
        o_hi, o_lo = sem("o_hi"), sem("o_lo")
        g_sig, g_sum = sem("g_sig"), sem("g_sum")
        dve_step, pool_step = sem("dve_step"), sem("pool_step")
        stored, slot_granted = sem("stored"), sem("slot_granted")

        def tiles(i):
            return NT if i < SUBS - 2 else LT

        def htiles(i):
            return NT if i < SUBS - 1 else LT

        def post0(i):
            return sum(tiles(j) for j in range(i))

        def pre0(i):
            return sum(htiles(j) for j in range(i))

        def width(i):
            return tiles(i) * P

        def mid(l):
            return TOK if l < DEPTH - 1 else SEQ

        ffns = [i for i in range(SUBS) if i % 3 != 1]

        def ff0(i):
            return KF * ffns.index(i)

        def stage0(i):
            return sum(KF if j % 3 != 1 else KD for j in range(i))

        IN_A = 28
        r_items = [[(h, s) for h in range(RH) for s in range(2 if l < DEPTH - 1 else 1)] for l in range(DEPTH)]
        n_items = [[(h, s, q) for h in range(NH) for s in range(2 if l < DEPTH - 1 else 1) for q in range(LT)]
                   for l in range(DEPTH)]
        f_items = [[(gr, s) for gr in range(FG) for s in range(2 if l < DEPTH - 1 else 1)] for l in range(DEPTH)]
        r0 = [0, len(r_items[0])]
        n0 = [0, len(n_items[0])]
        f0 = [0, len(f_items[0])]
        N_CONST = 17

        def streams(i):
            return 2 if tiles(i) == NT else 1

        def gate0(i):
            return sum(streams(j) for j in range(i))

        def key_n(item):
            return TOK if item[1] == 0 else CTX

        def loop(eng, n):
            if n == 1:
                class One:
                    def __enter__(self):
                        return 0

                    def __exit__(self, *a):
                        return False
                return One()
            return eng.Fori(0, n)

        block = ctx.enter_context(nc.Block())

        @block.sync
        def _(sp):
            def unit(u0, src, i=0, step=0):
                if u0 >= RING:
                    sp.wait_ge(w_split, i * step + (u0 - RING + 1))
                    if step:
                        sp.sem_inc(slot_granted, 1)
                s = u0 % RING
                k = src.shape[1]
                sp.dma_start(raw[:, s, :].rearrange("p (k n) -> p k n", k=k), src).then_inc(loaded[s], 16)

            def rows(w, c0, n, k0=0, k1=KD):
                return w[k0 * P:k1 * P, bass.ds(c0, n)].rearrange("(k p) n -> p k n", p=P)

            def ada_group(u0, s, gi, i=0, step=0):
                w = io["ada_w"][s // 3]
                for j in range(ADA_U):
                    unit(u0[j], rows(w, (s % 3) * 3 * D + gi * 512, 512, 2 * j, 2 * j + 2), i, step)

            for dst, name in ((ident, "k_ident"), (flip, "k_flip"), (swap, "k_swap"), (ropeC, "k_rope_c"),
                              (ropeS, "k_rope_s"), (dft_d, "k_dft_d"), (dft_n, "k_dft_n"), (wmask, "k_wmask"),
                              (sel, "k_sel"), (selb, "k_selb")):
                sp.dma_start(dst[:], io[name]).then_inc(const_in, 16)
            sp.dma_start(c2[:, 0, :], io["c"].rearrange("a (k p) -> p (a k)", p=P), allow_slow_non_contiguous=True).then_inc(const_in, 16)
            sp.dma_start(c2[:, 1, :], io["c_ctx"].rearrange("(k p) -> p k", p=P), allow_slow_non_contiguous=True).then_inc(const_in, 16)
            for l in range(DEPTH):
                sp.dma_start(gnw[:, l, :], io["ret_gn_w"][l].rearrange("(k p) -> p k", p=P), allow_slow_non_contiguous=True).then_inc(const_in, 16)
                sp.dma_start(gnb[:, l, :], io["ret_gn_b"][l].rearrange("(k p) -> p k", p=P), allow_slow_non_contiguous=True).then_inc(const_in, 16)
            sp.dma_start(lgt[:], io["ret_decay_logit"].rearrange("l d h -> (l d h)").partition_broadcast(P)).then_inc(const_in, 16)
            for j in range(ADA_U):
                unit(j, rows(io["ada_w"][0], 0, 512, 2 * j, 2 * j + 2))
            for t in range(LT):
                sp.dma_start(x[:, t, :], io["x"][0, t * P:(t + 1) * P, :]).then_inc(x_in, 16)
                sp.dma_start(x[:, LT + t, :], io["ctx"][0, t * P:(t + 1) * P, :]).then_inc(x_in, 16)
            with loop(sp, ADA_G - 1) as i:
                ada_group([ADA_U + j for j in range(ADA_U)], 0, i + 1, i, ADA_U)

            def ln_params(i, T):
                lnw, lnb = T[0], T[1]
                if i % 3 == 1:
                    sp.wait_ge(unit_done, AT["wo", i // 3])
                elif i >= 1:
                    sp.wait_ge(ff_mul, 2 + ff0(i) + 1)
                sp.dma_start(lnw[:], io["ln_w"][i // 3, i % 3].partition_broadcast(P)).then_inc(ln_in, 16)
                sp.dma_start(lnb[:], io["ln_b"][i // 3, i % 3].partition_broadcast(P)).then_inc(ln_in, 16)

            def ffn(i):
                l, w = i // 3, "ffa" if i % 3 == 0 else "ffb"
                w1, w3, w2 = io[w + "_w1"][l], io[w + "_w3"][l], io[w + "_w2"][l]
                u = AT["w13", i]
                it0 = 0
                if i + 1 < SUBS:
                    with loop(sp, ADA_IT) as k:
                        ada = io["ada_w"][(i + 1) // 3]
                        for j in range(2):
                            for o, ww in ((0, w1), (1, w3)):
                                unit(u + 4 * j + o, rows(ww, k * 256 + j * P, P), k, 8)
                            for o in range(2):
                                a = 2 * j + o
                                unit(u + 4 * j + 2 + o, rows(ada, ((i + 1) % 3) * 3 * D + k * 512, 512, 2 * a, 2 * a + 2), k, 8)
                    u += 8 * ADA_IT
                    it0 = ADA_IT
                with loop(sp, FFN_IT - it0) as k:
                    for j in range(2):
                        for o, ww in ((0, w1), (1, w3)):
                            unit(u + 2 * j + o, rows(ww, (k + it0) * 256 + j * P, P), k, 4)
                ln_params(i, T_ffn)
                u = AT["w2", i]
                for k0 in range(KF % 4):
                    unit(u + k0, w2[k0 * P:(k0 + 1) * P, :].rearrange("(k p) n -> p k n", p=P))
                u += KF % 4
                with loop(sp, KF // 4) as k:
                    for j in range(4):
                        unit(u + j, w2[bass.ds(k * 512 + (KF % 4 + j) * P, P), :].rearrange("(k p) n -> p k n", p=P), k, 4)

            def mixer(l):
                i = 3 * l + 1
                win = io["mix_w_in"][l]
                u = AT["ret_in", l]
                for gi, c0 in enumerate((C_RG, C_RG + 512, C_RK, C_RQ)):
                    for j in range(4):
                        unit(u + 8 * gi + 2 * j, rows(win, c0 + j * P, P))
                        unit(u + 8 * gi + 2 * j + 1, rows(io["ada_w"][l], 2 * 3 * D + gi * 512, 512, 2 * j, 2 * j + 2))
                for k in range(KD):
                    unit(AT["rv", l] + k, rows(win, C_RV, D, k, k + 1))
                for j in range(4):
                    unit(AT["fu", l] + j, rows(win, C_FU + j * P, P))
                u = AT["na_in", l]
                for gi, c0 in enumerate((C_NK, C_NQ)):
                    for j in range(4):
                        unit(u + 8 * gi + 2 * j, rows(win, c0 + j * P, P))
                        unit(u + 8 * gi + 2 * j + 1, rows(io["ada_w"][l], 2 * 3 * D + (4 + gi) * 512, 512, 2 * j, 2 * j + 2))
                for j in range(4):
                    unit(AT["nv", l] + j, rows(win, C_NV, 512, 2 * j, 2 * j + 2))
                u = AT["merge", l]
                with loop(sp, 2) as k:
                    for mm in range(4):
                        c = k * 512 + mm * P
                        v = u + 5 * mm
                        unit(v, rows(win, c + C_GT, P), k, 20)
                        unit(v + 1, rows(io["ret_w_out"][l], c, P), k, 20)
                        unit(v + 2, rows(win, c + (C_GT + D), P), k, 20)
                        unit(v + 3, rows(io["na_fou_w_out"][l], c, P), k, 20)
                        unit(v + 4, rows(win, c + (C_GT + 2 * D), P), k, 20)
                for k in range(KD):
                    unit(AT["wo", l] + k, rows(io["mix_w_o"][l], 0, D, k, k + 1))
                ln_params(i, T_mix)

            for l in range(DEPTH):
                ffn(3 * l)
                mixer(l)
                ffn(3 * l + 2)
            for t in range(LT):
                sp.wait_ge(x_ready, post0(SUBS - 1) + t + 1)
                sp.dma_start(out[0, t * P:(t + 1) * P, :], x[:, t, :]).then_inc(stored, 16)
            sp.wait_ge(stored, 16 * LT)

        @block.scalar
        def _(act):
            A = nc.scalar

            def rounded(u0, i=0, step=0):
                if u0 >= END:
                    return
                s = u0 % RING
                act.wait_ge(loaded[s], i * (16 * step // RING) + 16 * (u0 // RING + 1))
                if u0 >= RING:
                    act.wait_ge(unit_done, i * step + (u0 - RING + 1))
                A.activation(wh[:, s, :], raw[:, s, :], ACT.Copy).then_inc(w_rounded, 1)

            def load_mod_bias(s):
                act.wait_ge(mod_zero, s + 1)
                for r in (0, 2):
                    c0 = (s % 3) * 3 * D
                    act.dma_start(mod4[r:r + 1, :], io["ada_b"][s // 3:s // 3 + 1, c0:c0 + 3 * D]).then_inc(mod_bias, 16)

            def norm(i, tB):
                def pre_scale(t):
                    act.wait_ge(pre_rstd, pre0(i) + t + 1)
                    A.activation(tB[:, t], x[:, t], ACT.Identity, scale=mv[:, 1, t, 2:3],
                                 bias=mv[:, 1, t, 3:4]).then_inc(pre_norm, 1)

                def modulate(t):
                    act.wait_ge(h_turned, pre0(i) + t + 1)
                    y = ps[:, 2 * t:2 * t + 2].rearrange("p a n -> p (a n)").rearrange("p (k n) -> p k n", k=KD)
                    s = t // LT
                    for k in range(KD):
                        ins = A.activation(tB[:, t, k * P:(k + 1) * P], y[:, k], ACT.Identity, scale=modT[:, 1, k, s:s + 1],
                                           bias=modT[:, 0, k, s:s + 1])
                    ins.then_inc(h_mod, 1)

                def round_h(t):
                    act.wait_ge(h_mod, pre0(i) + t + 1)
                    A.activation(hh[:, :, t * P:(t + 1) * P], tB[:, t].rearrange("p (k n) -> p k n", k=KD),
                                 ACT.Copy).then_inc(h_hi, 1)

                act.wait_ge(mods_ready, i + 1)
                for t in range(htiles(i) + 1):
                    if t < htiles(i):
                        pre_scale(t)
                    if t >= 1:
                        modulate(t - 1)
                        round_h(t - 1)

            def form_b(i, u, src, n, ready, base, per):
                N = width(i)

                def stage(k0, k=0, looped=False):
                    act.wait_ge(ready, k * (4 * per) + (base + per * (k0 + 1)))
                    act.wait_ge(unit_done, k * 4 + (u + k0 - 1))
                    A.activation(sh_[:, k0 % 2, 0:N], src[:, bass.ds(k * 4 + k0, 1), 0:N] if looped else src[:, k0, 0:N],
                                 ACT.Copy).then_inc(stage_hi, 1)

                stage(0)
                stage(1)
                if i + 2 < SUBS:
                    load_mod_bias(i + 2)
                steps = min((n - 2) // 4, (END - RING - u) // 4)
                with loop(act, steps) as k:
                    for j in range(4):
                        rounded(u + 4 + j, k, 4)
                        stage(2 + j, k, steps > 1)
                for k0 in range(steps * 4, n):
                    rounded(u + 4 + k0)
                    if k0 + 2 < n:
                        stage(k0 + 2)

            def ffn(i):
                N = htiles(i) * P
                u, m = AT["w13", i], ff0(i)

                def sig(v, mt, k, step, j):
                    act.wait_ge(unit_done, k * step + (v + 1))
                    act.wait_ge(ff_mul, k * 2 + (mt + 1))
                    A.activation(T_ffn[3][:, j, 0:N], ps[:, 2 * j, 0:N], ACT.Sigmoid).then_inc(ff_sig, 1)

                it0 = 0
                if i + 1 < SUBS:
                    with loop(act, ADA_IT) as k:
                        for j in range(2):
                            v = u + 4 * j
                            rounded(v + 4, k, 8)
                            sig(v, m + j, k, 8, j)
                            for o in range(1, 4):
                                rounded(v + 4 + o, k, 8)
                    u += 8 * ADA_IT
                    m += 2 * ADA_IT
                    it0 = ADA_IT
                with loop(act, FFN_IT - it0) as k:
                    for j in range(2):
                        v = u + 2 * j
                        rounded(v + 4, k, 4)
                        sig(v, m + j, k, 4, j)
                        rounded(v + 5, k, 4)
                form_b(i, AT["w2", i], g, KF, ff_mul, 2 + ff0(i), 1)

            def load_bias(l, h):
                if h >= 2:
                    act.wait_ge(n_max, n0[l] + len(n_items[l]) // NH * (h - 1))
                for r in range(ROWS):
                    row = (l * NH + h) * RPB_R + 7 - r
                    src = bass.AP(tab.tensor, offset=row * TAB, ap=[[1, GRID_W], [TAB, ROWS], [1, GRID_W]])
                    part = (r % 2) * GRID_W
                    act.dma_start(bias[part:part + GRID_W, h % 2, r // 2, :].rearrange("p (r c) -> p r c", r=ROWS), src)\
                       .then_inc(bias_in[h % 2], 16)

            def retention(l):
                def decay(h):
                    f, b = 2 * l * RH + h, (2 * l + 1) * RH + h
                    act.wait_ge(dec_arg, RH * l + h + 1)
                    if RH * l + h >= 1:
                        act.wait_ge(dec_ready, RH * l + h)
                    A.activation(dec[:, h % 2, 0:2], dec[:, h % 2, 0:2], ACT.Exp)
                    A.activation(dec2[:], dist[:, 2], ACT.Exp, scale=small[:, 7, f:f + 1])
                    A.activation(dec[:, h % 2, 2:4], dist[:, 3], ACT.Exp, scale=small[:, 7, b:b + 1]).then_inc(dec_exp, 1)

                items, b = r_items[l], r0[l]
                per = len(items) // RH
                act.wait_ge(lg_ready, 1)
                decay(0)
                for t in range(len(items)):
                    if t % per == 0 and t // per + 1 < RH:
                        decay(t // per + 1)
                    act.wait_ge(r_out, b + t + 1)
                    if t >= 2:
                        act.wait_ge(r_fin, b + t - 1)
                    A.copy(ro[:, t % 2], ps[:, 4 + t % 2].rearrange("p (a n) -> p a n", a=2)).then_inc(r_copied, 1)
                    act.wait_ge(r_cent, b + t + 1)
                    if t >= 1:
                        act.wait_ge(r_var, b + t)
                    A.activation(rq2[:], ro[:, t % 2], ACT.Square).then_inc(r_sq, 1)

            def attention(l, N):
                items, b = n_items[l], n0[l]
                per = len(items) // NH
                for t in range(len(items) + 4):
                    if 1 <= t <= len(items):
                        v = t - 1
                        n = key_n(items[v])
                        act.wait_ge(n_turn, b + v + 1)
                        if v >= 2:
                            act.wait_ge(n_out, b + v - 1)
                        A.copy(probT[:, v % 2, 0:n], ps[:, 2 + v % 2, 0:n]).then_inc(n_turnc, 1)
                    if t < len(items):
                        if t % per == 0 and 2 <= t // per + 1 < NH:
                            load_bias(l, t // per + 1)
                        n = key_n(items[t])
                        act.wait_ge(n_max, b + t + 1)
                        if t >= 2:
                            act.wait_ge(n_turn, b + t - 1)
                        A.activation(prob[:, t % 2, 0:n], ps[:, t % 2, 0:n], ACT.Exp, bias=nmax[:, t % 2, 1:2],
                                     accum_out=nmax[:, t % 2, 2:3]).then_inc(n_exp, 1)
                    if t >= 3 and (t - 2) % (2 * per) == 0:
                        pr = (t - 2) // (2 * per) - 1
                        act.wait_ge(n_out, b + 2 * per * (pr + 1))
                        A.copy(ah[:, pr, 0:N], ps[:, 4 + pr % 2, 0:N]).then_inc(n_hi, 1)

            def mixer(l):
                i, N = 3 * l + 1, mid(l)
                u = AT["ret_in", l]
                with loop(act, 4) as k:
                    for j in range(8):
                        rounded(u + 4 + j, k, 8)
                act.dma_start(dist[:], io["k_dist"]).then_inc(dist_in, 16)
                for p in range(4):
                    act.wait_ge(in_copied, 4 + IN_A * l + 2 * p + 2)
                    if p >= 2:
                        act.wait_ge(rg_silu, 4 * l + p - 1)
                    A.activation(rp[:, p % 2].rearrange("p a n -> p (a n)").rearrange("p (a n) -> p a n", a=2)[:, :, 0:N],
                                 rgz[:, 2 * p:2 * p + 2, 0:N], ACT.Sigmoid).then_inc(rg_sig, 1)
                u = AT["rv", l]
                for k in range(KD):
                    rounded(u + 4 + k)
                for t in range(NT):
                    act.wait_ge(unit_done, u + KD)
                    A.copy(rv[:, t], ps[:, 2 * t:2 * t + 2].rearrange("p a n -> p (a n)")).then_inc(rv_copied, 1)
                retention(l)
                u = AT["fu", l]
                for j in range(4):
                    rounded(u + 4 + j)
                for t, (gr, s) in enumerate(f_items[l]):
                    act.wait_ge(f_two, f0[l] + t + 1)
                    A.copy(fh[:, gr, s * SEQ:(s + 1) * SEQ], ps[:, 6 + t % 2, 0:SEQ]).then_inc(f_hi, 1)
                u = AT["na_in", l]
                act.wait_ge(r_fin, r0[l] + len(r_items[l]))
                for h in range(2):
                    load_bias(l, h)
                with loop(act, 2) as k:
                    for j in range(8):
                        rounded(u + 4 + j, k, 8)
                u = AT["nv", l]
                for j in range(4):
                    rounded(u + 4 + j)
                for t in range(NT):
                    act.wait_ge(unit_done, u + 4)
                    A.copy(nv[:, t], ps[:, t]).then_inc(nv_copied, 1)
                attention(l, N)
                for p in range(2):
                    A.copy(oh[:, 4 * p:4 * p + 4, 0:N], rgz[:, 4 * p:4 * p + 4, 0:N]).then_inc(o_hi, 1)
                u = AT["merge", l]

                def gate(v, k, mm, w):
                    act.wait_ge(unit_done, k * 20 + (v + 2 * w + 1))
                    act.wait_ge(g_sum, k * 20 + (40 * l + 5 * mm + 2 * w + 1))
                    A.activation(sg[:, w, 0:N], ps[:, (0, 2, 5)[w], 0:N], ACT.Sigmoid).then_inc(g_sig, 1)

                with loop(act, 2) as k:
                    for mm in range(4):
                        v = u + 5 * mm
                        rounded(v + 4, k, 20)
                        gate(v, k, mm, 0)
                        rounded(v + 5, k, 20)
                        rounded(v + 6, k, 20)
                        gate(v, k, mm, 1)
                        rounded(v + 7, k, 20)
                        rounded(v + 8, k, 20)
                        gate(v, k, mm, 2)
                form_b(i, AT["wo", l], rgz, KD, g_sum, 5 + 40 * l, 5)

            act.sem_inc(g_sig, 3)
            act.wait_ge(pad_zero, 1)
            for l in range(DEPTH):
                act.dma_start(pad[:, l, 48:48 + RPB_C], io["na_rpb"][l].rearrange("h r c -> (h r) c")).then_inc(pad_in, 16)
            load_mod_bias(0)
            act.wait_ge(const_in, 16 * N_CONST)
            A.activation(c2s[:], c2[:], ACT.Sigmoid).then_inc(c_sig, 1)
            act.wait_ge(c_silu, 1)
            act.wait_ge(tables_set, 1)
            for s in range(2):
                A.activation(cs[:, :, 2 * s], c2[:, s, :], ACT.Copy).then_inc(c_hi, 1)
            for u in range(RING):
                rounded(u)
            act.wait_ge(pad_in, 16 * DEPTH)
            for l in range(DEPTH):
                act.dma_start(tab[l].rearrange("h r c -> (h r) c"), pad[:, l, :]).then_inc(tab_in, 16)
            A.activation(small[:, 0], lgt[:], ACT.Abs).then_inc(lg_abs, 1)
            act.wait_ge(lg_abs, 1)
            A.activation(small[:, 1], small[:, 0], ACT.Exp, scale=-1.0).then_inc(lg_exp, 1)
            with loop(act, ADA_G) as i:
                for j in range(ADA_U):
                    rounded(RING + j, i, ADA_U)
            load_mod_bias(1)
            act.wait_ge(tab_in, 16 * DEPTH)
            norm(0, T_ffn[4])
            for l in range(DEPTH):
                ffn(3 * l)
                norm(3 * l + 1, T_ffn[4])
                mixer(l)
                norm(3 * l + 2, T_mix[4])
                ffn(3 * l + 2)
                if 3 * l + 3 < SUBS:
                    norm(3 * l + 3, T_ffn[4])

        @block.gpsimd
        def _(pool):
            G = nc.gpsimd

            steps = [0]

            def link(ins):
                steps[0] += 1
                ins.then_inc(pool_step, 1)
                pool.wait_ge(pool_step, steps[0])

            def rstd(which, t, done):
                m = mv[:, which, t]
                link(G.tensor_scalar(m[:, 1:2], m[:, 1:2], EPS, None, ALU.add))
                ins = G.tensor_tensor(m[:, 2:3], m[:, 1:2], nhalf[:, 0:1], ALU.pow)
                if which == 0:
                    ins.then_inc(done, 1)
                    return
                link(ins)
                link(G.tensor_tensor(m[:, 3:4], m[:, 0:1], m[:, 2:3], ALU.mult))
                G.tensor_scalar(m[:, 3:4], m[:, 3:4], -1.0, None, ALU.mult).then_inc(done, 1)

            def norm(i, post, pre):
                npost, npre = tiles(i - 1) if post else 0, htiles(i) if pre else 0
                for t in range(max(npost, npre) + 1):
                    if t < npost:
                        pool.wait_ge(post_stat, post0(i - 1) + t + 1)
                        rstd(0, t, post_rstd)
                    if 1 <= t <= npre:
                        pool.wait_ge(pre_stat, pre0(i) + t)
                        rstd(1, t - 1, pre_rstd)

            G.memset(pad, 0.0).then_inc(pad_zero, 1)
            G.memset(cs[:].bitcast(F32), 0.0)
            G.memset(mean256[:], 1.0 / DV)
            G.memset(nhalf[:], -0.5).then_inc(tables_set, 1)
            norm(0, False, True)
            for l in range(DEPTH):
                norm(3 * l + 1, True, True)
                for t in range(len(r_items[l])):
                    pool.wait_ge(r_vare, r0[l] + t + 1)
                    G.tensor_tensor(rve[:, t % 2], rve[:, t % 2], nhalf[:], ALU.pow).then_inc(r_rstd, 1)
                for h in range(NH):
                    pool.wait_ge(bias_in[h % 2], 16 * ROWS * (l * NH // 2 + h // 2 + 1))
                    b = bias[:, h % 2].rearrange("p q (r c) -> p (q r) c", c=GRID_W)
                    G.tensor_tensor(b, b, wmask[:].unsqueeze(1).broadcast_to([P, LT * ROWS, GRID_W]), ALU.add)\
                     .then_inc(bias_masked, 1)
                norm(3 * l + 2, True, True)
                norm(3 * l + 3, True, 3 * l + 3 < SUBS)

        @block.vector
        def _(dve):
            V = nc.vector
            steps = [0]

            def link(ins):
                steps[0] += 1
                ins.then_inc(dve_step, 1)
                dve.wait_ge(dve_step, steps[0])

            def f(ap):
                return ap.bitcast(F32)

            def split(u0, i=0, step=0):
                if u0 >= END:
                    return
                dve.wait_ge(w_rounded, i * step + (u0 + 1))
                s = u0 % RING
                V.tensor_tensor(wl[:, s, :], raw[:, s, :], f(wh[:, s, :]), ALU.subtract).then_inc(w_split, 1)

            def ada_add(s, gi, u_last, k=0, ustep=0):
                dve.wait_ge(mod_bias, 32 * (s + 1))
                dve.wait_ge(unit_done, k * ustep + (u_last + 1))
                cols = mod4[:, bass.ds(k * 512 + gi * 512, 512)] if ustep else mod4[:, gi * 512:(gi + 1) * 512]
                V.tensor_tensor(cols, cols, ps[0:4, 4, :], ALU.add).then_inc(ada_sum, 1)

            def prepare(i, scale):
                if i >= 0:
                    T = T_mix if i % 3 == 1 else T_ffn
                    for s in range(streams(i)):
                        dve.wait_ge(gate_mm, gate0(i) + s + 1)
                        V.tensor_scalar(T[2][:, s], ps[:, 5:7].rearrange("p a n -> p (a n)"), scale, None, ALU.mult)\
                         .then_inc(gate_ready, 1)
                if i + 1 < SUBS:
                    dve.wait_ge(mods_mm, i + 2)
                    V.tensor_copy(modT[:, 0], ps[:, 7, 0:2 * KD].rearrange("p (k s) -> p k s", s=2))
                    V.tensor_scalar(modT[:, 1], ps[:, 7, 2 * KD:4 * KD].rearrange("p (k s) -> p k s", s=2), 1.0, None,
                                    ALU.add).then_inc(mods_ready, 1)
                    link(V.tensor_copy(grow[:], mod4[:, 2 * D:3 * D]))
                    V.memset(mod4[:], 0.0).then_inc(mod_zero, 1)

            def norm(i, T, post, pre, y_done):
                lnw, lnb, gateB, tA, tB = T
                npost, npre = tiles(i - 1) if post else 0, htiles(i) if pre else 0
                if post:
                    dve.wait_ge(ln_in, 32 * i)

                def stats(src, which, t, done):
                    for k in range(2):
                        ins = V.bn_stats(st[:, which, t, 6 * k:6 * k + 6], src[:, k * 512:(k + 1) * 512])
                    link(ins)
                    V.bn_aggr(mv[:, which, t, 0:2], st[:, which, t, 0:12]).then_inc(done, 1)

                def residual(t):
                    a = tA[:, t % 2]
                    dve.wait_ge(unit_done, y_done)
                    link(V.tensor_tensor(a, ps[:, 2 * t:2 * t + 2].rearrange("p a n -> p (a n)"), gateB[:, t // LT], ALU.mult))
                    link(V.scalar_tensor_tensor(out=a, in0=x[:, t], scalar=ALPHA, in1=a, op0=ALU.mult, op1=ALU.add))
                    stats(a, 0, t, post_stat)

                def affine(t):
                    a = tA[:, t % 2]
                    dve.wait_ge(post_rstd, post0(i - 1) + t + 1)
                    link(V.scalar_tensor_tensor(out=a, in0=a, scalar=mv[:, 0, t, 0:1], in1=lnw[:], op0=ALU.subtract, op1=ALU.mult))
                    V.scalar_tensor_tensor(out=x[:, t], in0=a, scalar=mv[:, 0, t, 2:3], in1=lnb[:], op0=ALU.mult,
                                           op1=ALU.add).then_inc(x_ready, 1)
                    dve.wait_ge(x_ready, post0(i - 1) + t + 1)

                def rest(t):
                    dve.wait_ge(h_hi, pre0(i) + t + 1)
                    V.tensor_tensor(hl[:, :, t * P:(t + 1) * P], tB[:, t].rearrange("p (k n) -> p k n", k=KD),
                                    f(hh[:, :, t * P:(t + 1) * P]), ALU.subtract).then_inc(h_lo, 1)

                for t in range(max(npost, npre) + 3):
                    if t < npost:
                        residual(t)
                    if 1 <= t <= max(npost, npre):
                        if post:
                            affine(t - 1)
                        if t <= npre:
                            stats(x[:, t - 1], 1, t - 1, pre_stat)
                    if 3 <= t <= npre + 2:
                        rest(t - 3)

            def form_b(i, u, src, n):
                N, b = width(i), stage0(i)

                def stage(k0, k=0, looped=False):
                    dve.wait_ge(stage_hi, k * 4 + (b + k0 + 1))
                    V.tensor_tensor(sl_[:, k0 % 2, 0:N], src[:, bass.ds(k * 4 + k0, 1), 0:N] if looped else src[:, k0, 0:N],
                                    f(sh_[:, k0 % 2, 0:N]), ALU.subtract).then_inc(stage_lo, 1)

                stage(0)
                stage(1)
                prepare(i, 0.5 if i % 3 != 1 else 1.0)
                steps_ = min((n - 2) // 4, (END - RING - u) // 4)
                with loop(dve, steps_) as k:
                    for j in range(4):
                        split(u + 4 + j, k, 4)
                        stage(2 + j, k, steps_ > 1)
                for k0 in range(steps_ * 4, n):
                    split(u + 4 + k0)
                    if k0 + 2 < n:
                        stage(k0 + 2)

            def ffn(i):
                N = htiles(i) * P
                u, m = AT["w13", i], ff0(i)

                def mul(v, mt, row, k, step, j):
                    sgb = T_ffn[3][:, j, 0:N]
                    split(v + 4, k, step)
                    dve.wait_ge(ff_sig, k * 2 + (mt + 1))
                    V.tensor_tensor(sgb, sgb, ps[:, 2 * j, 0:N], ALU.mult).then_inc(ff_gate, 1)
                    split(v + 5, k, step)
                    dve.wait_ge(ff_gate, k * 2 + (mt + 1))
                    dve.wait_ge(unit_done, k * step + (v + 2))
                    V.tensor_tensor(g[:, bass.ds(k * 2 + row, 1), 0:N], sgb, ps[:, 2 * j + 1, 0:N], ALU.mult).then_inc(ff_mul, 1)

                it0 = 0
                if i + 1 < SUBS:
                    with loop(dve, ADA_IT) as k:
                        for j in range(2):
                            mul(u + 4 * j, m + j, j, k, 8, j)
                            split(u + 4 * j + 6, k, 8)
                            split(u + 4 * j + 7, k, 8)
                        ada_add(i + 1, 0, u + 7, k, 8)
                    u += 8 * ADA_IT
                    it0 = ADA_IT
                with loop(dve, FFN_IT - it0) as k:
                    for j in range(2):
                        mul(u + 2 * j, m + 2 * it0 + j, 2 * it0 + j, k, 4, j)
                form_b(i, AT["w2", i], g, KF)

            def rope(l):
                for k in range(8):
                    t = kq[:, k, 0:SEQ]
                    dve.wait_ge(rope_mm, 8 * l + k + 1)
                    V.tensor_tensor(rq2[:, k % 2], ps[:, 5 + k % 2, 0:SEQ], ropeS[:], ALU.mult)
                    link(V.tensor_tensor(t, t, ropeC[:], ALU.mult))
                    V.tensor_tensor(t, t, rq2[:, k % 2], ALU.add).then_inc(rope_done, 1)

            def retention(l):
                items, b = r_items[l], r0[l]
                per = len(items) // RH

                def dec_first(h):
                    ff_, bb = 2 * l * RH + h, (2 * l + 1) * RH + h
                    d = dec[:, h % 2, 0:2]
                    link(V.tensor_scalar(d, dist[:, 0], small[:, 7, ff_:ff_ + 1], None, ALU.mult))
                    V.scalar_tensor_tensor(out=d, in0=dist[:, 1], scalar=small[:, 7, bb:bb + 1], in1=d, op0=ALU.mult,
                                           op1=ALU.add).then_inc(dec_arg, 1)

                def probs(t):
                    h, s = items[t]
                    if t % per == 0:
                        dve.wait_ge(dec_exp, RH * l + h + 1)
                        V.tensor_tensor(dec[:, h % 2, 2:4], dec[:, h % 2, 2:4], dec2[:], ALU.add).then_inc(dec_ready, 1)
                        dve.wait_ge(dec_ready, RH * l + h + 1)
                    n = 4 if s == 0 else 2
                    dve.wait_ge(r_score, b + t + 1)
                    if t >= 2:
                        dve.wait_ge(r_out, b + t - 1)
                    y = ps[:, 2 * (t % 2):2 * (t % 2) + n // 2].rearrange("p a (c n) -> p (a c) n", n=SEQ)
                    V.scalar_tensor_tensor(out=rp[:, t % 2, 0:n], in0=y, scalar=float(DK ** -0.5), in1=dec[:, h % 2, 0:n],
                                           op0=ALU.mult, op1=ALU.mult).then_inc(r_prob, 1)
                    if t % per == 0 and h + 1 < RH:
                        dec_first(h + 1)

                def centre(t):
                    dve.wait_ge(r_mean, b + t + 1)
                    for a in range(2):
                        ins = V.tensor_tensor(ro[:, t % 2, a], ro[:, t % 2, a], ps[:, 6, 0:SEQ], ALU.subtract)
                    ins.then_inc(r_cent, 1)

                def variance(t):
                    dve.wait_ge(r_var, b + t + 1)
                    V.tensor_scalar(rve[:, t % 2], ps[:, 6, SEQ:SEQ + LT], EPS, None, ALU.add).then_inc(r_vare, 1)

                def diagonal(t):
                    dve.wait_ge(r_rstd, b + t + 1)
                    for q in range(LT):
                        ins = V.tensor_scalar(rr[:, t % 2, q], ident[:], rve[:, t % 2, q:q + 1], float(DV), ALU.mult, ALU.mult)
                    ins.then_inc(r_diag, 1)

                def finish(t):
                    h, s = items[t]
                    dve.wait_ge(r_spread, b + t + 1)
                    dve.wait_ge(r_sq, b + t + 1)
                    o = ro[:, t % 2]
                    for a in range(2):
                        ins = V.tensor_tensor(o[:, a], o[:, a], ps[:, 7, 0:SEQ], ALU.mult)
                    link(ins)
                    for a in range(2):
                        k = 2 * h + a
                        ins = V.tensor_scalar(o[:, a], o[:, a], gnw[:, l, k:k + 1], gnb[:, l, k:k + 1], ALU.mult, ALU.add)
                    link(ins)
                    w = rgz[:, 2 * h:2 * h + 2, s * SEQ:(s + 1) * SEQ]
                    V.tensor_tensor(w, w, o, ALU.mult).then_inc(r_fin, 1)

                dve.wait_ge(dist_in, 16 * (l + 1))
                dec_first(0)
                probs(0)
                for t in range(len(items) + 1):
                    if t >= 1:
                        variance(t - 1)
                    if t + 1 < len(items):
                        probs(t + 1)
                    if t >= 1:
                        diagonal(t - 1)
                    if t < len(items):
                        centre(t)
                    if t >= 1:
                        finish(t - 1)

            def attention(l, N):
                items, b = n_items[l], n0[l]
                per = len(items) // NH

                def invert(t):
                    dve.wait_ge(n_exp, b + t + 1)
                    if t >= 2:
                        dve.wait_ge(n_turn, b + t - 1)
                    link(V.reciprocal(nmax[:, t % 2, 3:4], nmax[:, t % 2, 2:3]))
                    V.tensor_scalar(jd[:, t % 2], flip[:] if items[t][1] == 0 else ident[:], nmax[:, t % 2, 3:4], None,
                                    ALU.mult).then_inc(n_jd, 1)

                def maximum(t):
                    h, s, q = items[t]
                    dve.wait_ge(n_score, b + t + 1)
                    if s == 0:
                        if q == 0:
                            dve.wait_ge(bias_masked, NH * l + h + 1)
                        link(V.tensor_tensor(ps[:, t % 2, 0:SEQ], ps[:, t % 2, 0:SEQ], bias[:, h % 2, q], ALU.add))
                    link(V.tensor_reduce(nmax[:, t % 2, 0:1], ps[:, t % 2, 0:key_n(items[t])], AXX, ALU.max))
                    V.tensor_scalar(nmax[:, t % 2, 1:2], nmax[:, t % 2, 0:1], -1.0, None, ALU.mult).then_inc(n_max, 1)

                for t in range(len(items) + 4):
                    if 1 <= t <= len(items):
                        invert(t - 1)
                    if t < len(items):
                        maximum(t)
                    if t >= 3 and (t - 2) % (2 * per) == 0:
                        pr = (t - 2) // (2 * per) - 1
                        dve.wait_ge(n_hi, 4 * l + pr + 1)
                        V.tensor_tensor(al[:, pr, 0:N], ps[:, 4 + pr % 2, 0:N], f(ah[:, pr, 0:N]), ALU.subtract).then_inc(n_lo, 1)

            def copy_in(dst, u, idx, k=0, ustep=0, per=0, **kw):
                dve.wait_ge(unit_done, k * ustep + (u + 1))
                V.tensor_copy(dst, ps[:, idx % 4, 0:dst.shape[-1]]).then_inc(in_copied, 1)

            def mixer(l):
                i, N = 3 * l + 1, mid(l)
                s_next = i + 1
                u = AT["ret_in", l]
                for k0, n, w in ((0, 2, N), (2, 1, TOK), (3, 1, N)):
                    with loop(dve, n) as k:
                        for j in range(4):
                            row = 4 * k0 + j
                            dst = rgz[:, bass.ds(k * 4 + row, 1), 0:w] if n > 1 else kq[:, row - KD, 0:w]
                            split(u + 8 * k0 + 2 * j + 4, k, 8)
                            copy_in(dst, u + 8 * k0 + 2 * j, j, k, 8)
                            split(u + 8 * k0 + 2 * j + 5, k, 8)
                        ada_add(s_next, k0, u + 8 * k0 + 7, k, 8 if n > 1 else 0)
                for p in range(4):
                    dve.wait_ge(rg_sig, 4 * l + p + 1)
                    w = rgz[:, 2 * p:2 * p + 2, 0:N]
                    V.tensor_tensor(w, w, rp[:, p % 2].rearrange("p a n -> p (a n)").rearrange("p (a n) -> p a n", a=2)[:, :, 0:N],
                                    ALU.mult).then_inc(rg_silu, 1)
                rope(l)
                for k in range(KD):
                    split(AT["rv", l] + 4 + k)
                retention(l)
                for j in range(4):
                    split(AT["fu", l] + 4 + j)
                    copy_in(fu[:, j, 0:N], AT["fu", l] + j, j)
                for t in range(len(f_items[l]) + 1):
                    if t < len(f_items[l]):
                        dve.wait_ge(f_one, f0[l] + t + 1)
                        if t >= 2:
                            dve.wait_ge(f_two, f0[l] + t - 1)
                        V.tensor_copy(fA[:, t % 2], ps[:, 4 + t % 2].rearrange("p (a n) -> p a n", a=2)).then_inc(f_onec, 1)
                    if t >= 1:
                        gr, s = f_items[l][t - 1]
                        dve.wait_ge(f_hi, f0[l] + t)
                        V.tensor_tensor(fl[:, gr, s * SEQ:(s + 1) * SEQ], ps[:, 6 + (t - 1) % 2, 0:SEQ],
                                        f(fh[:, gr, s * SEQ:(s + 1) * SEQ]), ALU.subtract).then_inc(f_lo, 1)
                u = AT["na_in", l]
                for j in range(4):
                    split(u + 2 * j + 4)
                    copy_in(nkq[:, 0, j], u + 2 * j, j)
                    split(u + 2 * j + 5)
                ada_add(s_next, 4, u + 7)
                for j in range(4):
                    split(u + 8 + 2 * j + 4)
                    dve.wait_ge(unit_done, u + 8 + 2 * j + 1)
                    d = nkq[:, 1, j]
                    ins = V.tensor_scalar(d[:, 0:SEQ].rearrange("p (r c) -> p r c", c=GRID_W)[:, :, ::-1],
                                          ps[:, j, 0:SEQ].rearrange("p (r c) -> p r c", c=GRID_W), DH ** -0.5, None, ALU.mult)
                    if N > SEQ:
                        ins = V.tensor_scalar(d[:, SEQ:TOK], ps[:, j, SEQ:TOK], DH ** -0.5, None, ALU.mult)
                    ins.then_inc(in_copied, 1)
                    split(u + 8 + 2 * j + 5)
                ada_add(s_next, 5, u + 15)
                for j in range(4):
                    split(AT["nv", l] + 4 + j)
                attention(l, N)
                for p in range(2):
                    dve.wait_ge(o_hi, 2 * l + p + 1)
                    V.tensor_tensor(ol[:, 4 * p:4 * p + 4, 0:N], rgz[:, 4 * p:4 * p + 4, 0:N], f(oh[:, 4 * p:4 * p + 4, 0:N]),
                                    ALU.subtract).then_inc(o_lo, 1)
                dve.wait_ge(o_lo, 2 * l + 2)
                u = AT["merge", l]
                with loop(dve, 2) as k:
                    for mm in range(4):
                        v, q = u + 5 * mm, 5 + 40 * l + 5 * mm
                        z = rgz[:, bass.ds(k * 4 + mm, 1), 0:N]

                        def gated(w, out, bank, uu):
                            dve.wait_ge(g_sig, k * 12 + (3 + 24 * l + 3 * mm + w + 1))
                            dve.wait_ge(unit_done, k * 20 + (v + uu))
                            V.tensor_tensor(out, sg[:, w, 0:N], ps[:, bank, 0:N], ALU.mult).then_inc(g_sum, 1)

                        split(v + 4, k, 20)
                        split(v + 5, k, 20)
                        gated(0, z, 1, 2)
                        split(v + 6, k, 20)
                        split(v + 7, k, 20)
                        for n, (w, bank) in enumerate(((1, 3), (2, 4))):
                            if n:
                                split(v + 8, k, 20)
                            gated(w, sg[:, w, 0:N], bank, 4)
                            dve.wait_ge(g_sum, k * 20 + (q + 2 + 2 * n))
                            V.tensor_tensor(z, z, sg[:, w, 0:N], ALU.add).then_inc(g_sum, 1)
                            dve.wait_ge(g_sum, k * 20 + (q + 3 + 2 * n))
                form_b(i, AT["wo", l], rgz, KD)

            dve.sem_inc(ff_mul, 2)
            dve.sem_inc(in_copied, 4)
            dve.sem_inc(g_sum, 5)
            dve.sem_inc(ada_sum, 1)
            V.memset(mod4[:], 0.0).then_inc(mod_zero, 1)
            dve.wait_ge(c_sig, 1)
            V.tensor_tensor(c2[:], c2[:], c2s[:], ALU.mult).then_inc(c_silu, 1)
            for s in range(2):
                dve.wait_ge(c_hi, s + 1)
                V.tensor_tensor(cs[:, :, 2 * s + 1], c2[:, s, :], f(cs[:, :, 2 * s]), ALU.subtract).then_inc(c_lo, 1)
            for u in range(RING):
                split(u)
            dve.wait_ge(lg_exp, 1)
            link(V.tensor_scalar(small[:, 2], small[:, 1], 2.0, None, ALU.add))
            link(V.reciprocal(small[:, 3], small[:, 2]))
            link(V.tensor_tensor(small[:, 2], small[:, 1], small[:, 3], ALU.mult))
            link(V.tensor_tensor(small[:, 3], small[:, 2], small[:, 2], ALU.mult))
            link(V.tensor_scalar(small[:, 4], small[:, 3], 1.0 / 15, None, ALU.mult))
            for c in (13, 11, 9, 7, 5, 3):
                link(V.scalar_tensor_tensor(out=small[:, 4], in0=small[:, 4], scalar=1.0 / c, in1=small[:, 3],
                                            op0=ALU.add, op1=ALU.mult))
            link(V.tensor_scalar(small[:, 4], small[:, 4], 1.0, -2.0, ALU.add, ALU.mult))
            link(V.tensor_tensor(small[:, 4], small[:, 4], small[:, 2], ALU.mult))
            V.scalar_tensor_tensor(out=small[:, 7], in0=lgt[:], scalar=0.0, in1=small[:, 4], op0=ALU.min,
                                   op1=ALU.add).then_inc(lg_ready, 1)
            dve.wait_ge(lg_ready, 1)
            with loop(dve, ADA_G) as k:
                for j in range(ADA_U):
                    split(RING + j, k, ADA_U)
                ada_add(0, 0, ADA_U - 1, k, ADA_U)
            dve.wait_ge(x_in, 16 * NT)
            prepare(-1, 1.0)
            norm(0, T_ffn, False, True, 0)
            for l in range(DEPTH):
                ffn(3 * l)
                norm(3 * l + 1, T_ffn, True, True, AT["ret_in", l])
                mixer(l)
                norm(3 * l + 2, T_mix, True, True, AT["w13", 3 * l + 2])
                ffn(3 * l + 2)
                norm(3 * l + 3, T_ffn, True, 3 * l + 3 < SUBS, AT["w13", 3 * l + 3] if 3 * l + 3 < SUBS else END)

        @block.tensor
        def _(pe):
            T = nc.tensor

            def three(out, a, b, start, stop):
                T.matmul(out, a[0], b[0], start=start, stop=False)
                T.matmul(out, a[0], b[1], start=False, stop=False)
                return T.matmul(out, a[1], b[0], start=False, stop=stop)

            def ready(u, k=0, step=0):
                pe.wait_ge(w_split, k * step + (u + 1))

            def form_a(u, bank, src, n, k=0, step=0, kts=KD, row=0, last=True):
                s = u % RING
                if row == 0:
                    ready(u, k, step)
                for kt in range(kts):
                    c = (row + kt) * P
                    ins = three(ps[:, bank, 0:n], (wh[:, s, c:c + P], wl[:, s, c:c + P]),
                                (src[0][:, kt, 0:n], src[1][:, kt, 0:n]), kt == 0, kt == kts - 1)
                if last:
                    ins.then_inc(unit_done, 1)

            def ada(u, j, group, k=0, step=0):
                s = u % RING
                ready(u, k, step)
                if j == 0:
                    pe.wait_ge(ada_sum, (k if step else 0) + (group + 1))
                for a in range(2):
                    kt = 2 * j + a
                    T.matmul(ps[:, 4, :], cs[:, kt, :], wh[:, s, a * 512:(a + 1) * 512], start=kt == 0, stop=False)
                    ins = T.matmul(ps[:, 4, :], cs[:, kt, :], wl[:, s, a * 512:(a + 1) * 512], start=False, stop=kt == KD - 1)
                ins.then_inc(unit_done, 1)

            def prepare(i):
                if i >= 0:
                    for s in range(streams(i)):
                        if s:
                            pe.wait_ge(gate_ready, gate0(i) + s)
                        for a in range(2):
                            ins = T.matmul(ps[:, 5 + a, :], selb[:, s, :], grow[:, a * 512:(a + 1) * 512], start=True, stop=True)
                        ins.then_inc(gate_mm, 1)
                if i + 1 < SUBS:
                    pe.wait_ge(ada_sum, 1 + ADA_G * (i + 2))
                    for k in range(2 * KD):
                        ins = T.matmul(ps[:, 7, 2 * k:2 * k + 2], mod4[:, k * P:(k + 1) * P], sel[:], start=True, stop=True)
                    ins.then_inc(mods_mm, 1)

            def turn(i, tB):
                for t in range(htiles(i)):
                    pe.wait_ge(pre_norm, pre0(i) + t + 1)
                    for k in range(KD):
                        ins = T.transpose(ps[:, 2 * t + k // 4, (k % 4) * P:(k % 4 + 1) * P], tB[:, t, k * P:(k + 1) * P], ident[:])
                    ins.then_inc(h_turned, 1)
                pe.wait_ge(h_lo, pre0(i + 1))

            def form_b(i, u, n):
                b = stage0(i)

                def step(k0, k=0, first=False, last=False):
                    s = (u + k0) % RING
                    pe.wait_ge(w_split, k * 4 + (u + k0 + 1))
                    pe.wait_ge(stage_lo, k * 4 + (b + k0 + 1))
                    for t in range(tiles(i)):
                        a = (sh_[:, k0 % 2, t * P:(t + 1) * P], sl_[:, k0 % 2, t * P:(t + 1) * P])
                        for h in range(2):
                            w = slice(h * 512, (h + 1) * 512)
                            ins = three(ps[:, 2 * t + h, :], a, (wh[:, s, w], wl[:, s, w]), first, last)
                    ins.then_inc(unit_done, 1)

                head = (n - 1) % 4 or 4
                for k0 in range(head):
                    step(k0, first=k0 == 0)
                if n - 1 - head > 0:
                    with loop(pe, (n - 1 - head) // 4) as k:
                        for j in range(4):
                            step(head + j, k)
                step(n - 1, last=True)

            def ffn(i):
                N, u, m = htiles(i) * P, AT["w13", i], ff0(i)
                src = (hh, hl)

                def pair(v, mt, j, k, step):
                    pe.wait_ge(ff_mul, k * 2 + (mt + 1))
                    form_a(v, 2 * j, src, N, k, step)
                    form_a(v + 1, 2 * j + 1, src, N, k, step)

                it0 = 0
                if i + 1 < SUBS:
                    with loop(pe, ADA_IT) as k:
                        for j in range(2):
                            pair(u + 4 * j, m + j, j, k, 8)
                            for o in range(2):
                                ada(u + 4 * j + 2 + o, 2 * j + o, ADA_G * (i + 1), k, 8)
                    u += 8 * ADA_IT
                    it0 = ADA_IT
                with loop(pe, FFN_IT - it0) as k:
                    for j in range(2):
                        pair(u + 2 * j, m + 2 * it0 + j, j, k, 4)
                prepare(i)
                pe.wait_ge(ff_mul, 2 + m + KF)
                if i + 1 < SUBS:
                    pe.wait_ge(mods_ready, i + 2)
                pe.wait_ge(gate_ready, gate0(i + 1))
                form_b(i, AT["w2", i], KF)

            def token_form(u, n, width_):
                kt_per = UN // width_
                for k in range(n):
                    s = (u + k) % RING
                    ready(u + k)
                    for kk in range(kt_per):
                        kt = k * kt_per + kk
                        for t in range(NT):
                            a = (hh[:, kt, t * P:(t + 1) * P], hl[:, kt, t * P:(t + 1) * P])
                            for h in range(width_ // 512):
                                w = slice(kk * 512 + h * 512, kk * 512 + (h + 1) * 512)
                                ins = three(ps[:, t * (width_ // 512) + h, :], a, (wh[:, s, w], wl[:, s, w]),
                                            kt == 0, kt == KD - 1)
                    ins.then_inc(unit_done, 1)

            def retention(l):
                items, b = r_items[l], r0[l]

                def scores(t):
                    h, s = items[t]
                    if t >= 2:
                        pe.wait_ge(r_prob, b + t - 1)
                    for j, kt in enumerate(range(NT) if s == 0 else range(LT, NT)):
                        ins = T.matmul(ps[:, 2 * (t % 2) + j // 2, (j % 2) * SEQ:(j % 2 + 1) * SEQ],
                                       kq[:, h, kt * P:(kt + 1) * P], kq[:, 4 + h, s * SEQ:(s + 1) * SEQ],
                                       start=True, stop=True)
                    ins.then_inc(r_score, 1)

                def values(t):
                    h, s = items[t]
                    pe.wait_ge(r_prob, b + t + 1)
                    if t >= 2:
                        pe.wait_ge(r_copied, b + t - 1)
                    kts = list(range(NT) if s == 0 else range(LT, NT))
                    for a in range(2):
                        for j, kt in enumerate(kts):
                            c = h * DV + a * P
                            ins = T.matmul(ps[:, 4 + t % 2, a * SEQ:(a + 1) * SEQ], rv[:, kt, c:c + P], rp[:, t % 2, j],
                                           start=j == 0, stop=j == len(kts) - 1)
                    ins.then_inc(r_out, 1)

                def mean(t):
                    pe.wait_ge(r_copied, b + t + 1)
                    if t >= 1:
                        pe.wait_ge(r_cent, b + t)
                        pe.wait_ge(r_vare, b + t)
                    for a in range(2):
                        ins = T.matmul(ps[:, 6, 0:SEQ], mean256[:], ro[:, t % 2, a], start=a == 0, stop=a == 1)
                    ins.then_inc(r_mean, 1)

                def variance(t):
                    pe.wait_ge(r_sq, b + t + 1)
                    for q in range(LT):
                        for a in range(2):
                            ins = T.matmul(ps[:, 6, SEQ + q:SEQ + q + 1], rq2[:, a, q * P:(q + 1) * P], mean256[:, 0:1],
                                           start=a == 0, stop=a == 1)
                    ins.then_inc(r_var, 1)

                def spread(t):
                    pe.wait_ge(r_diag, b + t + 1)
                    if t >= 1:
                        pe.wait_ge(r_fin, b + t)
                    T.matmul(ps[:, 7, 0:SEQ], mean256[:], rr[:, t % 2].rearrange("p q n -> p (q n)"), start=True, stop=True)\
                     .then_inc(r_spread, 1)

                scores(0)
                for t in range(len(items) + 1):
                    if t < len(items):
                        values(t)
                    if t >= 1:
                        variance(t - 1)
                    if t + 1 < len(items):
                        scores(t + 1)
                    if t < len(items):
                        mean(t)
                    if t >= 1:
                        spread(t - 1)

            def attention(l):
                items, b = n_items[l], n0[l]
                per = len(items) // NH

                def scores(t):
                    h, s, q = items[t]
                    if t >= 2:
                        pe.wait_ge(n_exp, b + t - 1)
                    p0 = DH * (h % 2)
                    c = s * SEQ + q * P
                    T.matmul(ps[:, t % 2, 0:key_n(items[t])], nkq[p0:p0 + DH, 1, h // 2, c:c + P],
                             nkq[p0:p0 + DH, 0, h // 2, s * SEQ:TOK], start=True, stop=True).then_inc(n_score, 1)

                def turned(t):
                    pe.wait_ge(n_jd, b + t + 1)
                    if t >= 2:
                        pe.wait_ge(n_turnc, b + t - 1)
                    for j in range(key_n(items[t]) // P):
                        w = slice(j * P, (j + 1) * P)
                        ins = T.matmul(ps[:, 2 + t % 2, w], prob[:, t % 2, w], jd[:, t % 2], start=True, stop=True)
                    ins.then_inc(n_turn, 1)

                def values(t):
                    h, s, q = items[t]
                    pr = h // 2
                    pe.wait_ge(n_turnc, b + t + 1)
                    if t % (2 * per) == 0 and pr >= 2:
                        pe.wait_ge(n_lo, 4 * l + pr - 1)
                    p0, c = DH * (h % 2), s * SEQ + q * P
                    kts = list(range(NT) if s == 0 else range(LT, NT))
                    for j, kt in enumerate(kts):
                        ins = T.matmul(ps[p0:p0 + DH, 4 + pr % 2, c:c + P], nv[:, kt, h * DH:(h + 1) * DH],
                                       probT[:, t % 2, j * P:(j + 1) * P], start=j == 0, stop=j == len(kts) - 1)
                    ins.then_inc(n_out, 1)

                for t in range(len(items) + 2):
                    if t < len(items):
                        scores(t)
                    if 1 <= t <= len(items):
                        turned(t - 1)
                    if t >= 2:
                        values(t - 2)

            def mixer(l):
                i, N, src = 3 * l + 1, mid(l), (hh, hl)
                G0 = ADA_G * (i + 1)
                c0 = IN_A * l + 1

                def inputs(u, idx, n, gi, k=0, step=0):
                    for j in range(4):
                        pe.wait_ge(in_copied, k * 4 + (c0 + idx + j))
                        form_a(u + 2 * j, j, src, n, k, step)
                        ada(u + 2 * j + 1, j, G0 + gi, k, step)

                u = AT["ret_in", l]
                with loop(pe, 2) as k:
                    inputs(u, 0, N, 0, k, 8)
                inputs(u + 16, 8, TOK, 2)
                inputs(u + 24, 12, N, 3)
                for k in range(8):
                    pe.wait_ge(in_copied, c0 + 3 + 8 + k + 1)
                    if k >= 2:
                        pe.wait_ge(rope_done, 8 * l + k - 1)
                    T.matmul(ps[:, 5 + k % 2, 0:SEQ], swap[:], kq[:, k, 0:SEQ], start=True, stop=True).then_inc(rope_mm, 1)
                pe.wait_ge(in_copied, c0 + 3 + 16)
                pe.wait_ge(ada_sum, 1 + G0 + 4)
                pe.wait_ge(rope_done, 8 * (l + 1))
                token_form(AT["rv", l], KD, D)
                pe.wait_ge(rv_copied, NT * (l + 1))
                retention(l)
                pe.wait_ge(r_prob, r0[l] + len(r_items[l]))
                for j in range(4):
                    pe.wait_ge(in_copied, c0 + 16 + j)
                    form_a(AT["fu", l] + j, j, src, N)
                pe.wait_ge(in_copied, c0 + 3 + 20)
                pe.wait_ge(r_fin, r0[l] + len(r_items[l]))
                for t in range(len(f_items[l]) + 1):
                    if t < len(f_items[l]):
                        gr, s = f_items[l][t]
                        if t >= 2:
                            pe.wait_ge(f_onec, f0[l] + t - 1)
                        for a in range(2):
                            c = s * SEQ + a * P
                            ins = T.matmul(ps[:, 4 + t % 2, a * SEQ:(a + 1) * SEQ], fu[:, gr, c:c + P], dft_d[:], start=True, stop=True)
                        ins.then_inc(f_one, 1)
                    if t >= 1:
                        v = t - 1
                        pe.wait_ge(f_onec, f0[l] + v + 1)
                        if v >= 2:
                            pe.wait_ge(f_lo, f0[l] + v - 1)
                        for a in range(2):
                            for part in range(2):
                                ins = T.matmul(ps[:, 6 + v % 2, 0:SEQ], fA[:, v % 2, a, part * P:(part + 1) * P],
                                               dft_n[:, a, part, :], start=a + part == 0, stop=a + part == 2)
                        ins.then_inc(f_two, 1)
                u = AT["na_in", l]
                inputs(u, 20, TOK, 4)
                inputs(u + 8, 24, N, 5)
                pe.wait_ge(in_copied, c0 + 3 + IN_A)
                token_form(AT["nv", l], 4, 512)
                pe.wait_ge(nv_copied, NT * (l + 1))
                pe.wait_ge(ada_sum, 1 + G0 + 6)
                pe.wait_ge(f_lo, f0[l] + len(f_items[l]))
                attention(l)
                pe.wait_ge(n_lo, 4 * (l + 1))
                pe.wait_ge(o_lo, 2 * (l + 1))
                u = AT["merge", l]
                with loop(pe, 2) as k:
                    for mm in range(4):
                        v, sgn, smn = u + 5 * mm, 24 * l + 3 * mm, 40 * l + 5 * mm
                        pe.wait_ge(g_sig, k * 12 + (sgn + 1))
                        form_a(v, 0, src, N, k, 20)
                        pe.wait_ge(g_sum, k * 20 + (smn + 1))
                        form_a(v + 1, 1, (oh, ol), N, k, 20)
                        pe.wait_ge(g_sig, k * 12 + (sgn + 2))
                        form_a(v + 2, 2, src, N, k, 20)
                        pe.wait_ge(g_sum, k * 20 + (smn + 4))
                        form_a(v + 3, 3, (ah, al), N, k, 20, kts=4, last=False)
                        form_a(v + 3, 4, (fh, fl), N, k, 20, kts=4, row=4)
                        pe.wait_ge(g_sig, k * 12 + (sgn + 3))
                        form_a(v + 4, 5, src, N, k, 20)
                pe.wait_ge(g_sum, 5 + 40 * (l + 1))
                prepare(i)
                pe.wait_ge(mods_ready, i + 2)
                pe.wait_ge(gate_ready, gate0(i + 1))
                form_b(i, AT["wo", l], KD)

            pe.wait_ge(c_lo, 2)
            with loop(pe, ADA_G) as k:
                for j in range(ADA_U):
                    ada(j, j, 0, k, ADA_U)
            pe.wait_ge(const_in, 16 * N_CONST)
            pe.wait_ge(tables_set, 1)
            prepare(-1)
            turn(0, T_ffn[4])
            for l in range(DEPTH):
                ffn(3 * l)
                turn(3 * l + 1, T_ffn[4])
                mixer(l)
                turn(3 * l + 2, T_mix[4])
                ffn(3 * l + 2)
                if 3 * l + 3 < SUBS:
                    turn(3 * l + 3, T_ffn[4])


def constants():
    import numpy as np
    f32 = np.float32
    k = {"k_ident": np.eye(P, dtype=f32)}
    flip = np.zeros((P, P), f32)
    for r in range(P // GRID_W):
        for c in range(GRID_W):
            flip[r * GRID_W + GRID_W - 1 - c, r * GRID_W + c] = 1
    k["k_flip"] = flip
    swap = np.zeros((P, P), f32)
    C, S = np.zeros((P, SEQ), f32), np.zeros((P, SEQ), f32)
    pos = np.arange(SEQ)
    q = DK // 4
    freq = (f32(10000.0) ** (-np.arange(q, dtype=f32) / f32(q))).astype(f32)
    for half, p in enumerate((pos // GRID_W, pos % GRID_W)):
        ang = p.astype(f32)[None, :] * freq[:, None]
        for a in range(2):
            rows = slice(half * 2 * q + a * q, half * 2 * q + (a + 1) * q)
            C[rows], S[rows] = np.cos(ang), np.sin(ang)
        for j in range(q):
            m = half * 2 * q + j
            swap[m + q, m] = -1
            swap[m, m + q] = 1
    k["k_swap"], k["k_rope_c"], k["k_rope_s"] = swap, C, S
    d = np.arange(P)
    ang = 2 * np.pi * (np.outer(d, d) % P) / P
    k["k_dft_d"] = np.concatenate([np.cos(ang), np.sin(ang)], 1).astype(f32)
    n = np.arange(SEQ)
    ang = 2 * np.pi * (np.outer(n, n) % SEQ) / SEQ
    s = 1 / np.sqrt(SEQ * P)
    both = np.stack([np.cos(ang) * s, -np.sin(ang) * s], 1).astype(f32)
    k["k_dft_n"] = np.ascontiguousarray(both.reshape(2, P, 2, SEQ).transpose(1, 0, 2, 3))
    cq = GRID_W - 1 - np.arange(P) % GRID_W
    start = np.clip(cq - 8, 0, GRID_W - 16)
    ck = np.arange(GRID_W)
    inside = (ck[None] >= start[:, None]) & (ck[None] < start[:, None] + 16)
    k["k_wmask"] = np.where(inside, 0, -1e30).astype(f32)
    k["k_sel"] = np.array([[1, 0], [1, 0], [0, 1], [0, 1]], f32)
    k["k_selb"] = np.ascontiguousarray(np.broadcast_to(k["k_sel"][:, :, None], (4, 2, P)))
    key = (np.arange(2)[None, :, None] * P + np.arange(P)[:, None, None]).astype(f32)
    qry = np.arange(SEQ, dtype=f32)[None, None, :]
    k["k_dist"] = np.ascontiguousarray(np.stack([np.maximum(qry - key, 0), np.maximum(key - qry, 0),
                                                 qry + CTX - key, SEQ - qry + key], 1).astype(f32))
    return k


_INS = ['x', 'c', 'ctx', 'c_ctx', 'ada_w', 'ada_b', 'ln_w', 'ln_b', 'ffa_w1', 'ffa_w3', 'ffa_w2', 'mix_w_in',
        'ret_decay_logit', 'ret_gn_w', 'ret_gn_b', 'ret_w_out', 'na_rpb', 'mix_w_o',
        'ffb_w1', 'ffb_w3', 'ffb_w2']


def kernel(**inputs):
    import numpy as np
    import concourse.bacc as bacc
    from concourse.bass_utils import run_bass_kernel_spmd

    nc = bacc.Bacc("TRN2", target_bir_lowering=False, num_devices=1, dynamic_dma_scratch_size=512)
    arrays, io = {}, {}
    both = [("na_fou_w_out", np.concatenate([inputs["na_w_out"], inputs["fou_w_out"]], axis=1))]
    for name, a in [(n, inputs[n]) for n in _INS] + both + list(constants().items()):
        a = np.ascontiguousarray(a)
        arrays[f"in_{name}"] = a
        io[name] = nc.dram_tensor(f"in_{name}", a.shape, mybir.dt.from_np(a.dtype), kind="ExternalInput").ap()
    out = nc.dram_tensor("out_0", (1, SEQ, D), F32, kind="ExternalOutput").ap()
    trunk(nc, io, out)
    r = run_bass_kernel_spmd(nc, [arrays], core_ids=[0])
    return r.results[0]["out_0"]
```

```python
from contextlib import ExitStack

import concourse.bass as bass
from concourse import mybir

F32 = mybir.dt.float32
F32R = mybir.dt.float32r
ALU = mybir.AluOpType
ACT = mybir.ActivationFunctionType
AXX = mybir.AxisListType.X

P = 128
D = 1024
KD = D // P
SEQ = CTX = 256
TOK = SEQ + CTX
NT = TOK // P
LT = SEQ // P
DEPTH = 2
FF = 2816
KF = FF // P
GRID_W = 64
ROWS = SEQ // GRID_W
RH, DK, DV = 4, 128, 256
NH, DH = 8, 64
FG = 4
RPB_R, RPB_C = 15, 31
TAB = 128
EPS = 1e-6
ALPHA = float((2 * DEPTH) ** 0.25)

C_RQ, C_RK, C_RV, C_RG = 0, 512, 1024, 2048
C_NQ, C_NK, C_NV, C_FU, C_GT = 3072, 3584, 4096, 4608, 5120

RING = 4
TAIL = RING
UN = 1024
ADA_G = 6
ADA_U = 4
ADA_IT = 6
FFN_IT = KF // 2
SUBS = 3 * DEPTH

N_FFN_ADA = FFN_IT * 4 + ADA_IT * 4
N_FFN = FFN_IT * 4


def plan():
    at, u = {}, 0

    def put(name, n):
        nonlocal u
        at[name] = u
        u += n

    put("ada", ADA_G * ADA_U)
    for l in range(DEPTH):
        put(("w13", 3 * l), N_FFN_ADA)
        put(("w2", 3 * l), KF)
        put(("ret_in", l), 4 * 8)
        put(("rv", l), 8)
        put(("fu", l), 4)
        put(("na_in", l), 2 * 8)
        put(("nv", l), 4)
        put(("merge", l), 8 * 5)
        put(("wo", l), 8)
        put(("w13", 3 * l + 2), N_FFN_ADA if l < DEPTH - 1 else N_FFN)
        put(("w2", 3 * l + 2), KF)
    at["end"] = u
    return at


def trunk(nc, io, out):
    AT = plan()
    END = AT["end"]
    ctx = ExitStack()
    with ctx:
        def sem(name):
            return ctx.enter_context(nc.semaphore(name))

        def sb(name, shape, dt=F32, scope=ctx):
            return scope.enter_context(nc.sbuf_tensor(name, shape, dt))

        ps = ctx.enter_context(nc.psum_tensor("ps", [P, 8, 512], F32))

        x = sb("x_res", [P, NT, D])
        raw = sb("raw", [P, RING, UN])
        wh = sb("wh", [P, RING, UN], F32R)
        wl = sb("wl", [P, RING, UN], F32R)
        hh = sb("hh", [P, KD, TOK], F32R)
        hl = sb("hl", [P, KD, TOK], F32R)
        sh_ = sb("stage_h", [P, TAIL, TOK], F32R)
        sl_ = sb("stage_l", [P, TAIL, TOK], F32R)
        cs = sb("cs", [P, KD, 4], F32R)
        mod4 = sb("mod4", [36, 3 * D])

        modT = sb("modT", [P, 2, KD, 2])
        modL = sb("modL", [P, 2, KD, 2])
        ident = sb("ident", [P, P])
        flip = sb("flip", [P, P])
        swap = sb("swap", [P, P])
        ropeC = sb("ropeC", [P, SEQ])
        ropeS = sb("ropeS", [P, SEQ])
        dft_d = sb("dft_d", [P, 2 * P])
        dft_n = sb("dft_n", [P, 2, 2, SEQ])
        wmask = sb("wmask", [P, GRID_W])
        mean256 = sb("mean256", [P, P])
        selb = sb("selb", [36, 2, P])
        gnw = sb("gnw", [P, DEPTH, KD])
        gnb = sb("gnb", [P, DEPTH, KD])
        lgt = sb("lgt", [P, DEPTH * 2 * RH])
        small = sb("small", [P, 6, DEPTH * 2 * RH])
        c2 = sb("c2", [P, 2, KD])
        c2s = sb("c2s", [P, 2, KD])
        st = sb("st", [P, 2, 2, 12])
        mv = sb("mv", [P, 2, NT, 4])
        nhalf = sb("nhalf", [P, LT])
        vmean = sb("vmean", [P, 2, RH])
        rve = sb("rve", [P, 2, LT])
        nmax = sb("nmax", [P, 3, 4])

        def transition(scope):
            return (sb("lnw" + scope.tag, [P, D], scope=scope), sb("lnb" + scope.tag, [P, D], scope=scope),
                    sb("gateB" + scope.tag, [P, 2, D], scope=scope),
                    sb("tA" + scope.tag, [P, 2, D], scope=scope), sb("tB" + scope.tag, [P, NT, D], scope=scope))

        class Scope(ExitStack):
            tag = ""

        with Scope() as ffn:
            ffn.tag = "_f"
            g = sb("g", [P, KF, TOK], scope=ffn)
            T_ffn = transition(ffn)
            pad = T_ffn[3][0:NH * RPB_R, 0, 0:DEPTH * TAB].rearrange("p (l c) -> p l c", l=DEPTH)
        with Scope() as mix:
            rgz = sb("rgz", [P, KD, TOK], scope=mix)
            with Scope() as s:
                s.tag = "_m"
                T_mix = transition(s)
            with Scope() as s:
                kq = sb("kq", [P, 8, TOK], scope=s)
                rv = sb("rv", [P, NT, RH * DV], scope=s)
                dist = sb("dist", [P, 4, 2, SEQ], scope=s)
                dec = sb("dec", [P, 2, 4, SEQ], scope=s)
                dec2 = sb("dec2", [P, 2, SEQ], scope=s)
                rp = sb("rp", [P, 2, 4, SEQ], scope=s)
                ro = sb("ro", [P, 2, SEQ], scope=s)
                rq2 = sb("rq2", [P, 2, SEQ], scope=s)
                rsp = sb("rsp", [P, SEQ], scope=s)
                rr = sb("rr", [P, 2, LT, P], scope=s)
            fh = sb("fh", [P, FG, TOK], F32R, scope=mix)
            fl = sb("fl", [P, FG, TOK], F32R, scope=mix)
            ah = sb("ah", [P, FG, TOK], F32R, scope=mix)
            al = sb("al", [P, FG, TOK], F32R, scope=mix)
            with Scope() as s:
                fu = sb("fu", [P, FG, TOK], scope=s)
                fA = sb("fA", [P, 2, 2, 2 * P], scope=s)
            with Scope() as s:
                nkq = sb("nkq", [P, 2, 4, TOK], scope=s)
                nv = sb("nv", [P, NT, NH * DH], scope=s)
                bias = sb("bias", [P, 2, LT, SEQ], scope=s)
                prob = sb("prob", [P, 3, TOK], scope=s)
                probT = sb("probT", [P, 2, TOK], scope=s)
                jd = sb("jd", [P, 3, P], scope=s)
            with Scope() as s:
                oh = sb("oh", [P, KD, TOK], F32R, scope=s)
                ol = sb("ol", [P, KD, TOK], F32R, scope=s)
                sg = sb("sg", [P, 3, TOK], scope=s)
        tab = nc.dram_tensor("rpb_table", [DEPTH, NH, RPB_R, TAB], F32).ap()

        loaded = [sem(f"loaded{i}") for i in range(RING)]
        w_rounded, w_split, unit_done = sem("w_rounded"), sem("w_split"), sem("unit_done")
        c_in, ident_in, const_in, pad_zero, pad_in, tab_in, dist_in = [sem(n) for n in ("c_in", "ident_in", "const_in", "pad_zero", "pad_in", "tab_in", "dist_in")]
        x_in, tables_set, c_sig, c_silu, c_hi, c_lo = [sem(n) for n in ("x_in", "tables_set", "c_sig", "c_silu", "c_hi", "c_lo")]
        lg_abs, lg_exp, lg_ready = sem("lg_abs"), sem("lg_exp"), sem("lg_ready")
        mod_taken, mod_bias, ada_sum = sem("mod_taken"), sem("mod_bias"), sem("ada_sum")
        gate_mm, gate_ready, mods_mm, mods_ready = [sem(n) for n in ("gate_mm", "gate_ready", "mods_mm", "mods_ready")]
        y_tile, ln_in, post_stat, post_rstd, x_ready = [sem(n) for n in ("y_tile", "ln_in", "post_stat", "post_rstd", "x_ready")]
        pre_stat, pre_rstd, pre_norm, h_turned, h_mod, h_mod_last, h_hi, h_lo = [
            sem(n) for n in ("pre_stat", "pre_rstd", "pre_norm", "h_turned", "h_mod", "h_mod_last", "h_hi", "h_lo")]
        ff_sig, ff_gate, ff_mul = sem("ff_sig"), sem("ff_gate"), sem("ff_mul")
        stage_hi, stage_lo = sem("stage_hi"), sem("stage_lo")
        in_copied, rv_copied, nv_copied = sem("in_copied"), sem("rv_copied"), sem("nv_copied")
        rg_sig, rg_silu = sem("rg_sig"), sem("rg_silu")
        rope_mm, rope_done = sem("rope_mm"), sem("rope_done")
        dec_arg, dec_exp, dec_ready = sem("dec_arg"), sem("dec_exp"), sem("dec_ready")
        rv_tile, nv_tile, r_score, r_prob, r_out, r_sq, r_var, r_vare, r_rstd, r_diag, r_spread, r_taken, r_used, r_fin = [
            sem(n) for n in ("rv_tile", "nv_tile", "r_score", "r_prob", "r_out", "r_sq", "r_var", "r_vare", "r_rstd", "r_diag", "r_spread", "r_taken", "r_used", "r_fin")]
        f_one, f_onec, f_two, f_hi, f_lo = [sem(n) for n in ("f_one", "f_onec", "f_two", "f_hi", "f_lo")]
        bias_in = [sem(f"bias_in{i}") for i in range(2)]
        bias_masked = sem("bias_masked")
        n_score, n_max, n_exp, n_jd, n_turn, n_turnc, n_out, n_hi, n_lo = [
            sem(n) for n in ("n_score", "n_max", "n_exp", "n_jd", "n_turn", "n_turnc", "n_out", "n_hi", "n_lo")]
        o_hi, o_lo = sem("o_hi"), sem("o_lo")
        g_sig, g_sum = sem("g_sig"), sem("g_sum")
        dve_step, pool_step = sem("dve_step"), sem("pool_step")
        stored, slot_granted = sem("stored"), sem("slot_granted")

        def tiles(i):
            return NT if i < SUBS - 2 else LT

        def htiles(i):
            return NT if i < SUBS - 1 else LT

        def post0(i):
            return sum(tiles(j) for j in range(i))

        def pre0(i):
            return sum(htiles(j) for j in range(i))

        def y0(i):
            return sum(tiles(j) - 1 for j in range(i))

        def width(i):
            return tiles(i) * P

        def mid(l):
            return TOK if l < DEPTH - 1 else SEQ

        ffns = [i for i in range(SUBS) if i % 3 != 1]

        def ff0(i):
            return KF * ffns.index(i)

        def stage0(i):
            return sum(KF if j % 3 != 1 else KD for j in range(i))

        IN_A = 28
        r_items = [[(h, s) for h in range(RH) for s in range(2 if l < DEPTH - 1 else 1)] for l in range(DEPTH)]
        n_items = [[(h, s, q) for h in range(NH) for s in range(2 if l < DEPTH - 1 else 1) for q in range(LT)]
                   for l in range(DEPTH)]
        f_items = [[(gr, s) for gr in range(FG) for s in range(2 if l < DEPTH - 1 else 1)] for l in range(DEPTH)]
        r0 = [0, len(r_items[0])]
        n0 = [0, len(n_items[0])]
        f0 = [0, len(f_items[0])]
        N_CONST = 12

        def mod_bank(i):
            return 3 if i else 7

        SCORE_BANKS = (0, 1, 6)

        def streams(i):
            return 2 if tiles(i) == NT else 1

        def gate0(i):
            return sum(streams(j) for j in range(i))

        def early(l):
            return 2 // (len(r_items[l]) // RH)

        def key_n(item):
            return TOK if item[1] == 0 else CTX

        def loop(eng, n):
            if n == 1:
                class One:
                    def __enter__(self):
                        return 0

                    def __exit__(self, *a):
                        return False
                return One()
            return eng.Fori(0, n)

        def load_bias(queue, l, h):
            for r in range(ROWS):
                row = (l * NH + h) * RPB_R + 7 - r
                src = bass.AP(tab.tensor, offset=row * TAB, ap=[[1, GRID_W], [TAB, ROWS], [1, GRID_W]])
                part = (r % 2) * GRID_W
                queue.dma_start(bias[part:part + GRID_W, h % 2, r // 2, :].rearrange("p (r c) -> p r c", r=ROWS), src)\
                     .then_inc(bias_in[h % 2], 16)

        block = ctx.enter_context(nc.Block())

        @block.sync
        def _(sp):
            def unit(u0, src, i=0, step=0):
                if u0 >= RING:
                    sp.wait_ge(w_split, i * step + (u0 - RING + 1))
                    if step:
                        sp.sem_inc(slot_granted, 1)
                s = u0 % RING
                k = src.shape[1]
                sp.dma_start(raw[:, s, :].rearrange("p (k n) -> p k n", k=k), src).then_inc(loaded[s], 16)

            def rows(w, c0, n, k0=0, k1=KD):
                return w[k0 * P:k1 * P, bass.ds(c0, n)].rearrange("(k p) n -> p k n", p=P)

            def ada_group(u0, s, gi, i=0, step=0):
                w = io["ada_w"][s // 3]
                for j in range(ADA_U):
                    unit(u0[j], rows(w, (s % 3) * 3 * D + gi * 512, 512, 2 * j, 2 * j + 2), i, step)

            sp.dma_start(c2[:, 0, :], io["c"].rearrange("a (k p) -> p (a k)", p=P), allow_slow_non_contiguous=True).then_inc(c_in, 16)
            sp.dma_start(c2[:, 1, :], io["c_ctx"].rearrange("(k p) -> p k", p=P), allow_slow_non_contiguous=True).then_inc(c_in, 16)
            for j in range(ADA_U):
                unit(j, rows(io["ada_w"][0], 0, 512, 2 * j, 2 * j + 2))
            for t in range(LT):
                sp.dma_start(x[:, t, :], io["x"][0, t * P:(t + 1) * P, :]).then_inc(x_in, 16)
                sp.dma_start(x[:, LT + t, :], io["ctx"][0, t * P:(t + 1) * P, :]).then_inc(x_in, 16)
            for dst, name in ((ident[:], "k_ident"), (selb[32:36], "k_selb")):
                sp.dma_start(dst, io[name]).then_inc(ident_in, 16)
            with loop(sp, ADA_G - 1) as i:
                ada_group([ADA_U + j for j in range(ADA_U)], 0, i + 1, i, ADA_U)
            for dst, name in ((flip, "k_flip"), (swap, "k_swap"), (ropeC, "k_rope_c"), (ropeS, "k_rope_s"),
                              (dft_d, "k_dft_d"), (dft_n, "k_dft_n"), (wmask, "k_wmask")):
                sp.dma_start(dst[:], io[name]).then_inc(const_in, 16)
            for l in range(DEPTH):
                sp.dma_start(gnw[:, l, :], io["ret_gn_w"][l].rearrange("(k p) -> p k", p=P), allow_slow_non_contiguous=True).then_inc(const_in, 16)
                sp.dma_start(gnb[:, l, :], io["ret_gn_b"][l].rearrange("(k p) -> p k", p=P), allow_slow_non_contiguous=True).then_inc(const_in, 16)
            sp.dma_start(lgt[:], io["ret_decay_logit"].rearrange("l d h -> (l d h)").partition_broadcast(P)).then_inc(const_in, 16)

            def ln_params(i, T):
                lnw, lnb = T[0], T[1]
                if i % 3 == 1:
                    sp.wait_ge(unit_done, AT["wo", i // 3])
                elif i >= 1:
                    sp.wait_ge(ff_mul, 2 + ff0(i) + 1)
                sp.dma_start(lnw[:], io["ln_w"][i // 3, i % 3].partition_broadcast(P)).then_inc(ln_in, 16)
                sp.dma_start(lnb[:], io["ln_b"][i // 3, i % 3].partition_broadcast(P)).then_inc(ln_in, 16)

            def ffn(i):
                l, w = i // 3, "ffa" if i % 3 == 0 else "ffb"
                w1, w3, w2 = io[w + "_w1"][l], io[w + "_w3"][l], io[w + "_w2"][l]
                u = AT["w13", i]
                it0 = 0
                if i + 1 < SUBS:
                    with loop(sp, ADA_IT) as k:
                        ada = io["ada_w"][(i + 1) // 3]
                        for j in range(2):
                            for o, ww in ((0, w1), (1, w3)):
                                unit(u + 4 * j + o, rows(ww, k * 256 + j * P, P), k, 8)
                            for o in range(2):
                                a = 2 * j + o
                                unit(u + 4 * j + 2 + o, rows(ada, ((i + 1) % 3) * 3 * D + k * 512, 512, 2 * a, 2 * a + 2), k, 8)
                    u += 8 * ADA_IT
                    it0 = ADA_IT
                with loop(sp, FFN_IT - it0) as k:
                    for j in range(2):
                        for o, ww in ((0, w1), (1, w3)):
                            unit(u + 2 * j + o, rows(ww, (k + it0) * 256 + j * P, P), k, 4)
                ln_params(i, T_ffn)
                u = AT["w2", i]
                for k0 in range(KF % 4):
                    unit(u + k0, w2[k0 * P:(k0 + 1) * P, :].rearrange("(k p) n -> p k n", p=P))
                u += KF % 4
                with loop(sp, KF // 4) as k:
                    for j in range(4):
                        unit(u + j, w2[bass.ds(k * 512 + (KF % 4 + j) * P, P), :].rearrange("(k p) n -> p k n", p=P), k, 4)

            def mixer(l):
                i = 3 * l + 1
                win = io["mix_w_in"][l]
                u = AT["ret_in", l]
                for gi, c0 in enumerate((C_RG, C_RG + 512, C_RK, C_RQ)):
                    for j in range(4):
                        unit(u + 8 * gi + 2 * j, rows(win, c0 + j * P, P))
                        unit(u + 8 * gi + 2 * j + 1, rows(io["ada_w"][l], 2 * 3 * D + gi * 512, 512, 2 * j, 2 * j + 2))
                for k in range(KD):
                    unit(AT["rv", l] + k, rows(win, C_RV, D, k, k + 1))
                for j in range(4):
                    unit(AT["fu", l] + j, rows(win, C_FU + j * P, P))
                u = AT["na_in", l]
                for gi, c0 in enumerate((C_NK, C_NQ)):
                    for j in range(4):
                        unit(u + 8 * gi + 2 * j, rows(win, c0 + j * P, P))
                        unit(u + 8 * gi + 2 * j + 1, rows(io["ada_w"][l], 2 * 3 * D + (4 + gi) * 512, 512, 2 * j, 2 * j + 2))
                for j in range(4):
                    unit(AT["nv", l] + j, rows(win, C_NV, 512, 2 * j, 2 * j + 2))
                for h in range(2, NH):
                    sp.wait_ge(n_max, n0[l] + len(n_items[l]) // NH * (h - 1))
                    load_bias(sp, l, h)
                u = AT["merge", l]
                with loop(sp, 2) as k:
                    for mm in range(4):
                        c = k * 512 + mm * P
                        v = u + 5 * mm
                        unit(v, rows(win, c + C_GT, P), k, 20)
                        unit(v + 1, rows(io["ret_w_out"][l], c, P), k, 20)
                        unit(v + 2, rows(win, c + (C_GT + D), P), k, 20)
                        unit(v + 3, rows(io["na_fou_w_out"][l], c, P), k, 20)
                        unit(v + 4, rows(win, c + (C_GT + 2 * D), P), k, 20)
                for k in range(KD):
                    unit(AT["wo", l] + k, rows(io["mix_w_o"][l], 0, D, k, k + 1))
                ln_params(i, T_mix)

            for l in range(DEPTH):
                ffn(3 * l)
                mixer(l)
                ffn(3 * l + 2)
            for t in range(LT):
                sp.wait_ge(x_ready, post0(SUBS - 1) + t + 1)
                sp.dma_start(out[0, t * P:(t + 1) * P, :], x[:, t, :]).then_inc(stored, 16)
            sp.wait_ge(stored, 16 * LT)

        @block.scalar
        def _(act):
            A = nc.scalar

            def rounded(u0, i=0, step=0):
                if u0 >= END:
                    return
                s = u0 % RING
                act.wait_ge(loaded[s], i * (16 * step // RING) + 16 * (u0 // RING + 1))
                if u0 >= RING:
                    act.wait_ge(unit_done, i * step + (u0 - RING + 1))
                A.activation(wh[:, s, :], raw[:, s, :], ACT.Copy).then_inc(w_rounded, 1)

            def load_mod_bias(s):
                if s >= 1:
                    act.wait_ge(mod_taken, s)
                c0 = (s % 3) * 3 * D
                for row in range(4):
                    src = io["ada_b"][s // 3:s // 3 + 1, c0:c0 + 3 * D] if row % 2 == 0 else io["k_zero"]
                    act.dma_start(mod4[row:row + 1, :], src).then_inc(mod_bias, 16)

            def norm(i, tB, u):
                def pre_scale(t):
                    act.wait_ge(pre_rstd, pre0(i) + t + 1)
                    A.activation(tB[:, t], x[:, t], ACT.Identity, scale=mv[:, 1, t, 2:3],
                                 bias=mv[:, 1, t, 3:4]).then_inc(pre_norm, 1)

                def modulate(t):
                    act.wait_ge(h_turned, pre0(i) + t + 1)
                    y = ps[:, 2 * t:2 * t + 2].rearrange("p a n -> p (a n)").rearrange("p (k n) -> p k n", k=KD)
                    s = t // LT
                    for k in range(KD):
                        ins = A.activation(tB[:, t, k * P:(k + 1) * P], y[:, k], ACT.Identity, scale=modT[:, 1, k, s:s + 1],
                                           bias=modT[:, 0, k, s:s + 1])
                    ins.then_inc(h_mod, 1)

                def round_h(t):
                    if t < NT - 1:
                        act.wait_ge(h_mod, (NT - 1) * i + t + 1)
                    else:
                        act.wait_ge(h_mod_last, i + 1)
                    A.activation(hh[:, :, t * P:(t + 1) * P], tB[:, t].rearrange("p (k n) -> p k n", k=KD),
                                 ACT.Copy).then_inc(h_hi, 1)

                n = htiles(i)
                if i == 0:
                    for t in range(n):
                        pre_scale(t)
                    with loop(act, ADA_G) as k:
                        for j in range(ADA_U):
                            rounded(RING + j, k, ADA_U)
                else:
                    for t in range(LT):
                        pre_scale(t)
                        for j in range(2):
                            rounded(u + 2 * t + j)
                act.wait_ge(mods_ready, i + 1)
                for t in range(LT):
                    modulate(t)
                    round_h(t)
                if i > 0:
                    for t in range(LT, n):
                        pre_scale(t)
                for t in range(LT, n):
                    if t < NT - 1:
                        modulate(t)
                    round_h(t)
                if i + 1 < SUBS:
                    load_mod_bias(i + 1)

            def form_b(i, u, src, n, ready, base, per):
                N = width(i)

                def stage(k0, k=0, looped=False):
                    act.wait_ge(ready, k * (4 * per) + (base + per * (k0 + 1)))
                    if k0 >= TAIL:
                        act.wait_ge(unit_done, k * 4 + (u + k0 - TAIL + 1))
                    A.activation(sh_[:, k0 % TAIL, 0:N], src[:, bass.ds(k * 4 + k0, 1), 0:N] if looped else src[:, k0, 0:N],
                                 ACT.Copy).then_inc(stage_hi, 1)

                for k0 in range(TAIL):
                    stage(k0)
                steps = (n - TAIL) // 4
                with loop(act, steps) as k:
                    for j in range(4):
                        rounded(u + RING + j, k, 4)
                        stage(TAIL + j, k, steps > 1)
                for k0 in range(steps * 4, n - TAIL):
                    rounded(u + RING + k0)
                    stage(TAIL + k0)

            def ffn(i):
                N = htiles(i) * P
                u, m = AT["w13", i], ff0(i)

                def sig(v, mt, k, step, j):
                    act.wait_ge(unit_done, k * step + (v + 1))
                    act.wait_ge(ff_mul, k * 2 + (mt + 1))
                    A.activation(T_ffn[3][:, j, 0:N], ps[:, 2 * j, 0:N], ACT.Sigmoid).then_inc(ff_sig, 1)

                it0 = 0
                if i + 1 < SUBS:
                    with loop(act, ADA_IT) as k:
                        for j in range(2):
                            v = u + 4 * j
                            rounded(v + 4, k, 8)
                            sig(v, m + j, k, 8, j)
                            for o in range(1, 4):
                                rounded(v + 4 + o, k, 8)
                    u += 8 * ADA_IT
                    m += 2 * ADA_IT
                    it0 = ADA_IT
                with loop(act, FFN_IT - it0) as k:
                    for j in range(2):
                        v = u + 2 * j
                        rounded(v + 4, k, 4)
                        sig(v, m + j, k, 4, j)
                        rounded(v + 5, k, 4)
                form_b(i, AT["w2", i], g, KF, ff_mul, 2 + ff0(i), 1)

            def decay(l, h):
                f, b = 2 * l * RH + h, (2 * l + 1) * RH + h
                act.wait_ge(dec_arg, RH * l + h + 1)
                if RH * l + h >= 1:
                    act.wait_ge(dec_ready, RH * l + h)
                A.activation(dec[:, h % 2, 0:2], dec[:, h % 2, 0:2], ACT.Exp)
                A.activation(dec2[:], dist[:, 2], ACT.Exp, scale=small[:, 5, f:f + 1])
                A.activation(dec[:, h % 2, 2:4], dist[:, 3], ACT.Exp, scale=small[:, 5, b:b + 1]).then_inc(dec_exp, 1)

            def retention(l):
                items, b = r_items[l], r0[l]
                per = len(items) // RH
                for h in range(1, early(l)):
                    decay(l, h)
                for t in range(len(items)):
                    act.wait_ge(r_out, b + t + 1)
                    if t >= 1:
                        act.wait_ge(r_var, b + t)
                    A.activation(rq2[:], ps[:, 4 + t % 3].rearrange("p (a n) -> p a n", a=2), ACT.Square).then_inc(r_sq, 1)
                    if t + 2 < len(items) and (t + 2) % per == 0 and (t + 2) // per >= early(l):
                        decay(l, (t + 2) // per)

            def attention(l, N):
                items, b = n_items[l], n0[l]
                per = len(items) // NH
                for t in range(len(items) + 4):
                    if t < len(items):
                        n = key_n(items[t])
                        act.wait_ge(n_max, b + t + 1)
                        if t >= 3:
                            act.wait_ge(n_turn, b + t - 2)
                        A.activation(prob[:, t % 3, 0:n], ps[:, SCORE_BANKS[t % 3], 0:n], ACT.Exp, bias=nmax[:, t % 3, 1:2],
                                     accum_out=nmax[:, t % 3, 2:3]).then_inc(n_exp, 1)
                    if 2 <= t < len(items) + 2:
                        v = t - 2
                        n = key_n(items[v])
                        act.wait_ge(n_turn, b + v + 1)
                        if v >= 2:
                            act.wait_ge(n_out, b + v - 1)
                        A.copy(probT[:, v % 2, 0:n], ps[:, 2 + v % 2, 0:n]).then_inc(n_turnc, 1)
                    if 0 <= t - (len(items) - RING) < RING:
                        rounded(AT["merge", l] + t - (len(items) - RING))
                    if t >= 4 and (t - 3) % (2 * per) == 0:
                        pr = (t - 3) // (2 * per) - 1
                        act.wait_ge(n_out, b + 2 * per * (pr + 1))
                        A.copy(ah[:, pr, 0:N], ps[:, 4 + pr % 2, 0:N]).then_inc(n_hi, 1)

            def mixer(l):
                i, N = 3 * l + 1, mid(l)
                u = AT["ret_in", l]
                with loop(act, 4) as k:
                    for j in range(8):
                        rounded(u + 4 + j, k, 8)
                act.dma_start(dist[:], io["k_dist"]).then_inc(dist_in, 16)
                for p in range(4):
                    act.wait_ge(in_copied, 4 + IN_A * l + 2 * p + 2)
                    if p >= 2:
                        act.wait_ge(rg_silu, 4 * l + p - 1)
                    A.activation(rp[:, p % 2].rearrange("p a n -> p (a n)").rearrange("p (a n) -> p a n", a=2)[:, :, 0:N],
                                 rgz[:, 2 * p:2 * p + 2, 0:N], ACT.Sigmoid).then_inc(rg_sig, 1)
                act.wait_ge(lg_ready, 1)
                decay(l, 0)
                u = AT["rv", l]
                for k in range(KD):
                    rounded(u + 4 + k)
                retention(l)
                u = AT["fu", l]
                for j in range(4):
                    rounded(u + 4 + j)
                for t, (gr, s) in enumerate(f_items[l]):
                    act.wait_ge(f_two, f0[l] + t + 1)
                    A.copy(fh[:, gr, s * SEQ:(s + 1) * SEQ], ps[:, 6 + t % 2, 0:SEQ]).then_inc(f_hi, 1)
                u = AT["na_in", l]
                act.wait_ge(r_fin, r0[l] + len(r_items[l]))
                for h in range(2):
                    load_bias(act, l, h)
                with loop(act, 2) as k:
                    for j in range(8):
                        rounded(u + 4 + j, k, 8)
                u = AT["nv", l]
                for t in range(NT):
                    act.wait_ge(*((nv_tile, (NT - 1) * l + t + 1) if t < NT - 1 else (unit_done, u + 4)))
                    A.copy(nv[:, t], ps[:, t]).then_inc(nv_copied, 1)
                attention(l, N)
                for p in range(2):
                    A.copy(oh[:, 4 * p:4 * p + 4, 0:N], rgz[:, 4 * p:4 * p + 4, 0:N]).then_inc(o_hi, 1)
                u = AT["merge", l]

                def gate(v, k, mm, w):
                    act.wait_ge(unit_done, k * 20 + (v + 2 * w + 1))
                    act.wait_ge(g_sum, k * 20 + (40 * l + 5 * mm + 2 * w + 1))
                    A.activation(sg[:, w, 0:N], ps[:, (0, 2, 5)[w], 0:N], ACT.Sigmoid).then_inc(g_sig, 1)

                with loop(act, 2) as k:
                    for mm in range(4):
                        v = u + 5 * mm
                        rounded(v + 4, k, 20)
                        gate(v, k, mm, 0)
                        rounded(v + 5, k, 20)
                        rounded(v + 6, k, 20)
                        gate(v, k, mm, 1)
                        rounded(v + 7, k, 20)
                        rounded(v + 8, k, 20)
                        gate(v, k, mm, 2)
                form_b(i, AT["wo", l], rgz, KD, g_sum, 5 + 40 * l, 5)

            act.sem_inc(g_sig, 3)
            act.wait_ge(pad_zero, 1)
            for l in range(DEPTH):
                act.dma_start(pad[:, l, 48:48 + RPB_C], io["na_rpb"][l].rearrange("h r c -> (h r) c")).then_inc(pad_in, 16)
            load_mod_bias(0)
            act.wait_ge(c_in, 32)
            A.activation(c2s[:], c2[:], ACT.Sigmoid).then_inc(c_sig, 1)
            act.wait_ge(c_silu, 1)
            act.wait_ge(tables_set, 1)
            for s in range(2):
                A.activation(cs[:, :, 2 * s], c2[:, s, :], ACT.Copy).then_inc(c_hi, 1)
            for u in range(RING):
                rounded(u)

            norm(0, T_ffn[4], RING)
            act.wait_ge(pad_in, 16 * DEPTH)
            for l in range(DEPTH):
                act.dma_start(tab[l].rearrange("h r c -> (h r) c"), pad[:, l, :]).then_inc(tab_in, 16)
            act.wait_ge(tab_in, 16 * DEPTH)
            act.wait_ge(const_in, 16 * N_CONST)
            A.activation(small[:, 0], lgt[:], ACT.Abs).then_inc(lg_abs, 1)
            act.wait_ge(lg_abs, 1)
            A.activation(small[:, 1], small[:, 0], ACT.Exp, scale=-1.0).then_inc(lg_exp, 1)
            for l in range(DEPTH):
                ffn(3 * l)
                norm(3 * l + 1, T_ffn[4], AT["ret_in", l])
                mixer(l)
                norm(3 * l + 2, T_mix[4], AT["w13", 3 * l + 2])
                ffn(3 * l + 2)
                if 3 * l + 3 < SUBS:
                    norm(3 * l + 3, T_ffn[4], AT["w13", 3 * l + 3])

        @block.gpsimd
        def _(pool):
            G = nc.gpsimd

            steps = [0]

            def link(ins):
                steps[0] += 1
                ins.then_inc(pool_step, 1)
                pool.wait_ge(pool_step, steps[0])

            def rstd(which, t, done):
                m = mv[:, which, t]
                link(G.tensor_scalar(m[:, 1:2], m[:, 1:2], EPS, None, ALU.add))
                ins = G.tensor_tensor(m[:, 2:3], m[:, 1:2], nhalf[:, 0:1], ALU.pow)
                if which == 0:
                    ins.then_inc(done, 1)
                    return
                link(ins)
                link(G.tensor_tensor(m[:, 3:4], m[:, 0:1], m[:, 2:3], ALU.mult))
                G.tensor_scalar(m[:, 3:4], m[:, 3:4], -1.0, None, ALU.mult).then_inc(done, 1)

            def norm(i, post, pre):
                npost, npre = tiles(i - 1) if post else 0, htiles(i) if pre else 0
                for t in range(max(npost, npre) + 1):
                    if t < npost:
                        pool.wait_ge(post_stat, post0(i - 1) + t + 1)
                        rstd(0, t, post_rstd)
                    if 1 <= t <= npre:
                        pool.wait_ge(pre_stat, pre0(i) + t)
                        rstd(1, t - 1, pre_rstd)

            G.memset(pad, 0.0).then_inc(pad_zero, 1)
            G.memset(cs[:].bitcast(F32), 0.0)
            G.memset(mean256[:], 1.0 / DV)
            G.memset(nhalf[:], -0.5).then_inc(tables_set, 1)
            norm(0, False, True)
            for l in range(DEPTH):
                norm(3 * l + 1, True, True)
                for t in range(len(r_items[l])):
                    pool.wait_ge(r_vare, r0[l] + t + 1)
                    G.tensor_tensor(rve[:, t % 2], rve[:, t % 2], nhalf[:], ALU.pow).then_inc(r_rstd, 1)
                for h in range(NH):
                    pool.wait_ge(bias_in[h % 2], 16 * ROWS * (l * NH // 2 + h // 2 + 1))
                    b = bias[:, h % 2].rearrange("p q (r c) -> p (q r) c", c=GRID_W)
                    G.tensor_tensor(b, b, wmask[:].unsqueeze(1).broadcast_to([P, LT * ROWS, GRID_W]), ALU.add)\
                     .then_inc(bias_masked, 1)
                norm(3 * l + 2, True, True)
                norm(3 * l + 3, True, 3 * l + 3 < SUBS)

        @block.vector
        def _(dve):
            V = nc.vector
            steps = [0]

            def link(ins):
                steps[0] += 1
                ins.then_inc(dve_step, 1)
                dve.wait_ge(dve_step, steps[0])

            def f(ap):
                return ap.bitcast(F32)

            def split(u0, i=0, step=0):
                if u0 >= END:
                    return
                dve.wait_ge(w_rounded, i * step + (u0 + 1))
                s = u0 % RING
                V.tensor_tensor(wl[:, s, :], raw[:, s, :], f(wh[:, s, :]), ALU.subtract).then_inc(w_split, 1)

            def ada_add(s, gi, u_last, k=0, ustep=0):
                dve.wait_ge(mod_bias, 64 * (s + 1))
                dve.wait_ge(unit_done, k * ustep + (u_last + 1))
                cols = mod4[0:4, bass.ds(k * 512 + gi * 512, 512)] if ustep else mod4[0:4, gi * 512:(gi + 1) * 512]
                V.tensor_tensor(cols, cols, ps[0:4, 4, :], ALU.add).then_inc(ada_sum, 1)

            def gates(i, scale):
                T = T_mix if i % 3 == 1 else T_ffn
                for s in range(streams(i)):
                    dve.wait_ge(gate_mm, gate0(i) + s + 1)
                    V.tensor_scalar(T[2][:, s], ps[:, 6 - 2 * s:8 - 2 * s].rearrange("p a n -> p (a n)"), scale, None, ALU.mult)\
                     .then_inc(gate_ready, 1)

            def modulations(i):
                dve.wait_ge(mods_mm, i + 1)
                y = ps[:, mod_bank(i), 0:8 * KD].rearrange("p (w k s h) -> p w k s h", w=2, k=KD, s=2)
                V.tensor_copy(modT[:], y[:, :, :, :, 0])
                link(V.tensor_copy(modL[:], y[:, :, :, :, 1]))
                link(V.tensor_tensor(modT[:], modT[:], modL[:], ALU.add))
                V.tensor_scalar(modT[:, 1], modT[:, 1], 1.0, None, ALU.add).then_inc(mods_ready, 1)

            def take_gates(i):
                V.tensor_copy(mod4[32:36, 0:D], mod4[0:4, 2 * D:3 * D]).then_inc(mod_taken, 1)

            def norm(i, T, post, pre, y_done):
                lnw, lnb, gateB, tA, tB = T
                npost, npre = tiles(i - 1) if post else 0, htiles(i) if pre else 0
                if post:
                    dve.wait_ge(ln_in, 32 * i)

                def stats(src, which, t, done):
                    for k in range(2):
                        ins = V.bn_stats(st[:, which, t % 2, 6 * k:6 * k + 6], src[:, k * 512:(k + 1) * 512])
                    link(ins)
                    V.bn_aggr(mv[:, which, t, 0:2], st[:, which, t % 2, 0:12]).then_inc(done, 1)

                def residual(t):
                    a = tA[:, t % 2]
                    if t < tiles(i - 1) - 1:
                        dve.wait_ge(y_tile, y0(i - 1) + t + 1)
                    else:
                        dve.wait_ge(unit_done, y_done)
                    link(V.tensor_tensor(a, ps[:, 2 * t:2 * t + 2].rearrange("p a n -> p (a n)"), gateB[:, t // LT], ALU.mult))
                    link(V.scalar_tensor_tensor(out=a, in0=x[:, t], scalar=ALPHA, in1=a, op0=ALU.mult, op1=ALU.add))
                    stats(a, 0, t, post_stat)

                def affine(t):
                    a = tA[:, t % 2]
                    dve.wait_ge(post_rstd, post0(i - 1) + t + 1)
                    link(V.scalar_tensor_tensor(out=a, in0=a, scalar=mv[:, 0, t, 0:1], in1=lnw[:], op0=ALU.subtract, op1=ALU.mult))
                    V.scalar_tensor_tensor(out=x[:, t], in0=a, scalar=mv[:, 0, t, 2:3], in1=lnb[:], op0=ALU.mult,
                                           op1=ALU.add).then_inc(x_ready, 1)
                    dve.wait_ge(x_ready, post0(i - 1) + t + 1)

                def rest(t):
                    dve.wait_ge(h_hi, pre0(i) + t + 1)
                    V.tensor_tensor(hl[:, :, t * P:(t + 1) * P], tB[:, t].rearrange("p (k n) -> p k n", k=KD),
                                    f(hh[:, :, t * P:(t + 1) * P]), ALU.subtract).then_inc(h_lo, 1)

                def modulate(t):
                    dve.wait_ge(h_turned, pre0(i) + t + 1)
                    y = ps[:, 2 * t:2 * t + 2].rearrange("p a n -> p (a n)").rearrange("p (k n) -> p k n", k=KD)
                    s = t // LT
                    for k in range(KD):
                        ins = V.tensor_scalar(tB[:, t, k * P:(k + 1) * P], y[:, k], modT[:, 1, k, s:s + 1],
                                              modT[:, 0, k, s:s + 1], ALU.mult, ALU.add)
                    ins.then_inc(h_mod_last, 1)

                def front(t):
                    if post:
                        affine(t)
                    if pre and t < npre:
                        stats(x[:, t], 1, t, pre_stat)

                if i == 0:
                    dve.wait_ge(x_in, 16 * NT)
                    for t in range(npre):
                        front(t)
                    with loop(dve, ADA_G) as k:
                        for j in range(ADA_U):
                            split(RING + j, k, ADA_U)
                        ada_add(0, 0, ADA_U - 1, k, ADA_U)
                    modulations(0)
                    for t in range(LT):
                        rest(t)
                else:
                    u = y_done
                    residual(0)
                    residual(1)
                    front(0)
                    if npost > LT:
                        residual(2)
                    front(1)
                    if pre:
                        modulations(i)
                        split(u)
                        split(u + 1)
                    if npost > LT:
                        residual(3)
                    if pre:
                        split(u + 2)
                        split(u + 3)
                        for t in range(LT):
                            rest(t)
                    for t in range(LT, npost):
                        front(t)
                if npre > LT:
                    modulate(NT - 1)
                    for t in range(LT, npre):
                        rest(t)
                if pre:
                    take_gates(i)

            def form_b(i, u, src, n):
                N, b = width(i), stage0(i)

                def stage(k0, k=0, looped=False):
                    dve.wait_ge(stage_hi, k * 4 + (b + k0 + 1))
                    V.tensor_tensor(sl_[:, k0 % TAIL, 0:N], src[:, bass.ds(k * 4 + k0, 1), 0:N] if looped else src[:, k0, 0:N],
                                    f(sh_[:, k0 % TAIL, 0:N]), ALU.subtract).then_inc(stage_lo, 1)

                for k0 in range(TAIL):
                    stage(k0)
                    if k0 == 0 and i % 3 == 1:
                        gates(i, 1.0)
                steps_ = (n - TAIL) // 4
                with loop(dve, steps_) as k:
                    for j in range(4):
                        split(u + RING + j, k, 4)
                        stage(TAIL + j, k, steps_ > 1)
                for k0 in range(steps_ * 4, n - TAIL):
                    split(u + RING + k0)
                    stage(TAIL + k0)

            def ffn(i):
                N = htiles(i) * P
                u, m = AT["w13", i], ff0(i)

                def mul(v, mt, row, k, step, j):
                    sgb = T_ffn[3][:, j, 0:N]
                    split(v + 4, k, step)
                    dve.wait_ge(ff_sig, k * 2 + (mt + 1))
                    V.tensor_tensor(sgb, sgb, ps[:, 2 * j, 0:N], ALU.mult).then_inc(ff_gate, 1)
                    split(v + 5, k, step)
                    dve.wait_ge(ff_gate, k * 2 + (mt + 1))
                    dve.wait_ge(unit_done, k * step + (v + 2))
                    V.tensor_tensor(g[:, bass.ds(k * 2 + row, 1), 0:N], sgb, ps[:, 2 * j + 1, 0:N], ALU.mult).then_inc(ff_mul, 1)

                it0 = 0
                if i + 1 < SUBS:
                    with loop(dve, ADA_IT) as k:
                        for j in range(2):
                            mul(u + 4 * j, m + j, j, k, 8, j)
                            split(u + 4 * j + 6, k, 8)
                            split(u + 4 * j + 7, k, 8)
                        ada_add(i + 1, 0, u + 7, k, 8)
                    u += 8 * ADA_IT
                    it0 = ADA_IT
                gates(i, 0.5)
                with loop(dve, FFN_IT - it0) as k:
                    for j in range(2):
                        mul(u + 2 * j, m + 2 * it0 + j, 2 * it0 + j, k, 4, j)
                form_b(i, AT["w2", i], g, KF)

            def rope(l, k):
                t = kq[:, k, 0:SEQ]
                dve.wait_ge(rope_mm, 8 * l + k + 1)
                V.tensor_tensor(rq2[:, k % 2], ps[:, 5 + k % 2, 0:SEQ], ropeS[:], ALU.mult)
                link(V.tensor_tensor(t, t, ropeC[:], ALU.mult))
                V.tensor_tensor(t, t, rq2[:, k % 2], ALU.add).then_inc(rope_done, 1)

            def dec_first(l, h):
                ff_, bb = 2 * l * RH + h, (2 * l + 1) * RH + h
                d = dec[:, h % 2, 0:2]
                link(V.tensor_scalar(d, dist[:, 0], small[:, 5, ff_:ff_ + 1], None, ALU.mult))
                V.scalar_tensor_tensor(out=d, in0=dist[:, 1], scalar=small[:, 5, bb:bb + 1], in1=d, op0=ALU.mult,
                                       op1=ALU.add).then_inc(dec_arg, 1)

            def decays(l):
                dve.wait_ge(dist_in, 16 * (l + 1))
                for h in range(early(l)):
                    dec_first(l, h)

            def retention(l):
                items, b = r_items[l], r0[l]
                per = len(items) // RH

                def probs(t):
                    h, s = items[t]
                    if t % per == 0:
                        dve.wait_ge(dec_exp, RH * l + h + 1)
                        V.tensor_tensor(dec[:, h % 2, 2:4], dec[:, h % 2, 2:4], dec2[:], ALU.add).then_inc(dec_ready, 1)
                        dve.wait_ge(dec_ready, RH * l + h + 1)
                    n = 4 if s == 0 else 2
                    dve.wait_ge(r_score, b + t + 1)
                    if t >= 2:
                        dve.wait_ge(r_out, b + t - 1)
                    y = ps[:, 2 * (t % 2):2 * (t % 2) + n // 2].rearrange("p a (c n) -> p (a c) n", n=SEQ)
                    V.scalar_tensor_tensor(out=rp[:, t % 2, 0:n], in0=y, scalar=float(DK ** -0.5), in1=dec[:, h % 2, 0:n],
                                           op0=ALU.mult, op1=ALU.mult).then_inc(r_prob, 1)

                def variance(t):
                    dve.wait_ge(r_var, b + t + 1)
                    V.tensor_scalar(rve[:, t % 2], ps[:, 7, SEQ:SEQ + LT], EPS, None, ALU.add).then_inc(r_vare, 1)

                def diagonal(t):
                    dve.wait_ge(r_rstd, b + t + 1)
                    for q in range(LT):
                        ins = V.tensor_scalar(rr[:, t % 2, q], ident[:], rve[:, t % 2, q:q + 1], float(DV), ALU.mult, ALU.mult)
                    ins.then_inc(r_diag, 1)

                def scale(t):
                    dve.wait_ge(r_spread, b + t + 1)
                    V.tensor_copy(rsp[:], ps[:, 7, 0:SEQ]).then_inc(r_taken, 1)
                    dve.wait_ge(r_taken, b + t + 1)
                    dve.wait_ge(r_sq, b + t + 1)
                    for a in range(2):
                        ins = V.tensor_tensor(ro[:, a], ps[:, 4 + t % 3, a * SEQ:(a + 1) * SEQ], rsp[:], ALU.mult)
                    ins.then_inc(r_used, 1)
                    dve.wait_ge(r_used, b + t + 1)

                def finish(t):
                    h, s = items[t]
                    for a in range(2):
                        k = 2 * h + a
                        ins = V.tensor_scalar(ro[:, a], ro[:, a], gnw[:, l, k:k + 1], gnb[:, l, k:k + 1], ALU.mult, ALU.add)
                    link(ins)
                    w = rgz[:, 2 * h:2 * h + 2, s * SEQ:(s + 1) * SEQ]
                    V.tensor_tensor(w, w, ro[:], ALU.mult).then_inc(r_fin, 1)

                probs(0)
                for t in range(len(items) + 2):
                    if t >= 2:
                        scale(t - 2)
                    if t + 1 < len(items):
                        probs(t + 1)
                    if 1 <= t <= len(items):
                        variance(t - 1)
                    if t >= 2:
                        finish(t - 2)
                    if 1 <= t <= len(items):
                        diagonal(t - 1)
                    if t + 2 < len(items) and (t + 2) % per == 0 and (t + 2) // per >= early(l):
                        dec_first(l, (t + 2) // per)
                    if t % per == 0 and t < TAIL * per:
                        split(AT["rv", l] + KD + t // per)

            def attention(l, N):
                items, b = n_items[l], n0[l]
                per = len(items) // NH

                def invert(t):
                    dve.wait_ge(n_exp, b + t + 1)
                    if t >= 3:
                        dve.wait_ge(n_turn, b + t - 2)
                    link(V.reciprocal(nmax[:, t % 3, 3:4], nmax[:, t % 3, 2:3]))
                    V.tensor_scalar(jd[:, t % 3], flip[:] if items[t][1] == 0 else ident[:], nmax[:, t % 3, 3:4], None,
                                    ALU.mult).then_inc(n_jd, 1)

                def maximum(t):
                    h, s, q = items[t]
                    y = ps[:, SCORE_BANKS[t % 3]]
                    dve.wait_ge(n_score, b + t + 1)
                    if s == 0:
                        if q == 0:
                            dve.wait_ge(bias_masked, NH * l + h + 1)
                        link(V.tensor_tensor(y[:, 0:SEQ], y[:, 0:SEQ], bias[:, h % 2, q], ALU.add))
                    link(V.tensor_reduce(nmax[:, t % 3, 0:1], y[:, 0:key_n(items[t])], AXX, ALU.max))
                    V.tensor_scalar(nmax[:, t % 3, 1:2], nmax[:, t % 3, 0:1], -1.0, None, ALU.mult).then_inc(n_max, 1)

                for t in range(len(items) + 4):
                    if t < len(items):
                        maximum(t)
                    if 1 <= t <= len(items):
                        invert(t - 1)
                    if t >= 4 and (t - 3) % (2 * per) == 0:
                        pr = (t - 3) // (2 * per) - 1
                        dve.wait_ge(n_hi, 4 * l + pr + 1)
                        V.tensor_tensor(al[:, pr, 0:N], ps[:, 4 + pr % 2, 0:N], f(ah[:, pr, 0:N]), ALU.subtract).then_inc(n_lo, 1)
                    if 0 <= t - (len(items) - RING) < RING:
                        split(AT["merge", l] + t - (len(items) - RING))

            def copy_in(dst, u, idx, k=0, ustep=0, per=0, **kw):
                dve.wait_ge(unit_done, k * ustep + (u + 1))
                V.tensor_copy(dst, ps[:, idx % 4, 0:dst.shape[-1]]).then_inc(in_copied, 1)

            def mixer(l):
                i, N = 3 * l + 1, mid(l)
                s_next = i + 1
                u = AT["ret_in", l]
                for k0, n, w in ((0, 2, N), (2, 1, TOK), (3, 1, N)):
                    with loop(dve, n) as k:
                        for j in range(4):
                            row = 4 * k0 + j
                            dst = rgz[:, bass.ds(k * 4 + row, 1), 0:w] if n > 1 else kq[:, row - KD, 0:w]
                            split(u + 8 * k0 + 2 * j + 4, k, 8)
                            copy_in(dst, u + 8 * k0 + 2 * j, j, k, 8)
                            split(u + 8 * k0 + 2 * j + 5, k, 8)
                            if row > KD:
                                rope(l, row - KD - 1)
                        ada_add(s_next, k0, u + 8 * k0 + 7, k, 8 if n > 1 else 0)
                rope(l, 7)
                for p in range(4):
                    dve.wait_ge(rg_sig, 4 * l + p + 1)
                    w = rgz[:, 2 * p:2 * p + 2, 0:N]
                    V.tensor_tensor(w, w, rp[:, p % 2].rearrange("p a n -> p (a n)").rearrange("p (a n) -> p a n", a=2)[:, :, 0:N],
                                    ALU.mult).then_inc(rg_silu, 1)
                decays(l)
                u = AT["rv", l]
                for k in range(KD - TAIL):
                    split(u + 4 + k)
                for t in range(NT):
                    if t < NT - 1:
                        dve.wait_ge(rv_tile, (NT - 1) * l + t + 1)
                    else:
                        dve.wait_ge(unit_done, u + KD)
                    y = ps[:, 2 * t:2 * t + 2].rearrange("p a n -> p (a n)").rearrange("p (h n) -> p h n", h=RH)
                    m = vmean[:, t % 2]
                    link(V.tensor_reduce(m, y, AXX, ALU.add))
                    link(V.tensor_scalar(m, m, 1.0 / DV, None, ALU.mult))
                    V.tensor_tensor(rv[:, t].rearrange("p (h n) -> p h n", h=RH), y,
                                    m.unsqueeze(2).broadcast_to([P, RH, DV]), ALU.subtract).then_inc(rv_copied, 1)
                retention(l)
                for j in range(4):
                    split(AT["fu", l] + 4 + j)
                    copy_in(fu[:, j, 0:N], AT["fu", l] + j, j)
                for t in range(len(f_items[l]) + 1):
                    if t < len(f_items[l]):
                        dve.wait_ge(f_one, f0[l] + t + 1)
                        if t >= 2:
                            dve.wait_ge(f_two, f0[l] + t - 1)
                        V.tensor_copy(fA[:, t % 2], ps[:, 4 + t % 2].rearrange("p (a n) -> p a n", a=2)).then_inc(f_onec, 1)
                    if t >= 1:
                        gr, s = f_items[l][t - 1]
                        dve.wait_ge(f_hi, f0[l] + t)
                        V.tensor_tensor(fl[:, gr, s * SEQ:(s + 1) * SEQ], ps[:, 6 + (t - 1) % 2, 0:SEQ],
                                        f(fh[:, gr, s * SEQ:(s + 1) * SEQ]), ALU.subtract).then_inc(f_lo, 1)
                u = AT["na_in", l]
                for j in range(4):
                    split(u + 2 * j + 4)
                    copy_in(nkq[:, 0, j], u + 2 * j, j)
                    split(u + 2 * j + 5)
                ada_add(s_next, 4, u + 7)
                for j in range(4):
                    split(u + 8 + 2 * j + 4)
                    dve.wait_ge(unit_done, u + 8 + 2 * j + 1)
                    d = nkq[:, 1, j]
                    ins = V.tensor_scalar(d[:, 0:SEQ].rearrange("p (r c) -> p r c", c=GRID_W)[:, :, ::-1],
                                          ps[:, j, 0:SEQ].rearrange("p (r c) -> p r c", c=GRID_W), DH ** -0.5, None, ALU.mult)
                    if N > SEQ:
                        ins = V.tensor_scalar(d[:, SEQ:TOK], ps[:, j, SEQ:TOK], DH ** -0.5, None, ALU.mult)
                    ins.then_inc(in_copied, 1)
                    split(u + 8 + 2 * j + 5)
                ada_add(s_next, 5, u + 15)
                attention(l, N)
                for p in range(2):
                    dve.wait_ge(o_hi, 2 * l + p + 1)
                    V.tensor_tensor(ol[:, 4 * p:4 * p + 4, 0:N], rgz[:, 4 * p:4 * p + 4, 0:N], f(oh[:, 4 * p:4 * p + 4, 0:N]),
                                    ALU.subtract).then_inc(o_lo, 1)
                dve.wait_ge(o_lo, 2 * l + 2)
                u = AT["merge", l]
                with loop(dve, 2) as k:
                    for mm in range(4):
                        v, q = u + 5 * mm, 5 + 40 * l + 5 * mm
                        z = rgz[:, bass.ds(k * 4 + mm, 1), 0:N]

                        def gated(w, out, bank, uu):
                            dve.wait_ge(g_sig, k * 12 + (3 + 24 * l + 3 * mm + w + 1))
                            dve.wait_ge(unit_done, k * 20 + (v + uu))
                            V.tensor_tensor(out, sg[:, w, 0:N], ps[:, bank, 0:N], ALU.mult).then_inc(g_sum, 1)

                        split(v + 4, k, 20)
                        split(v + 5, k, 20)
                        gated(0, z, 1, 2)
                        split(v + 6, k, 20)
                        split(v + 7, k, 20)
                        for n, (w, bank) in enumerate(((1, 3), (2, 4))):
                            if n:
                                split(v + 8, k, 20)
                            gated(w, sg[:, w, 0:N], bank, 4)
                            dve.wait_ge(g_sum, k * 20 + (q + 2 + 2 * n))
                            V.tensor_tensor(z, z, sg[:, w, 0:N], ALU.add).then_inc(g_sum, 1)
                            dve.wait_ge(g_sum, k * 20 + (q + 3 + 2 * n))
                form_b(i, AT["wo", l], rgz, KD)

            dve.sem_inc(ff_mul, 2)
            dve.sem_inc(in_copied, 4)
            dve.sem_inc(g_sum, 5)
            dve.sem_inc(ada_sum, 1)
            dve.wait_ge(c_sig, 1)
            V.tensor_tensor(c2[:], c2[:], c2s[:], ALU.mult).then_inc(c_silu, 1)
            for s in range(2):
                dve.wait_ge(c_hi, s + 1)
                V.tensor_tensor(cs[:, :, 2 * s + 1], c2[:, s, :], f(cs[:, :, 2 * s]), ALU.subtract).then_inc(c_lo, 1)
            for u in range(RING):
                split(u)
            norm(0, T_ffn, False, True, 0)
            dve.wait_ge(lg_exp, 1)
            link(V.tensor_scalar(small[:, 2], small[:, 1], 2.0, None, ALU.add))
            link(V.reciprocal(small[:, 3], small[:, 2]))
            link(V.tensor_tensor(small[:, 2], small[:, 1], small[:, 3], ALU.mult))
            link(V.tensor_tensor(small[:, 3], small[:, 2], small[:, 2], ALU.mult))
            link(V.tensor_scalar(small[:, 4], small[:, 3], 1.0 / 15, None, ALU.mult))
            for c in (13, 11, 9, 7, 5, 3):
                link(V.scalar_tensor_tensor(out=small[:, 4], in0=small[:, 4], scalar=1.0 / c, in1=small[:, 3],
                                            op0=ALU.add, op1=ALU.mult))
            link(V.tensor_scalar(small[:, 4], small[:, 4], 1.0, -2.0, ALU.add, ALU.mult))
            link(V.tensor_tensor(small[:, 4], small[:, 4], small[:, 2], ALU.mult))
            V.scalar_tensor_tensor(out=small[:, 5], in0=lgt[:], scalar=0.0, in1=small[:, 4], op0=ALU.min,
                                   op1=ALU.add).then_inc(lg_ready, 1)
            dve.wait_ge(lg_ready, 1)
            for l in range(DEPTH):
                ffn(3 * l)
                norm(3 * l + 1, T_ffn, True, True, AT["ret_in", l])
                mixer(l)
                norm(3 * l + 2, T_mix, True, True, AT["w13", 3 * l + 2])
                ffn(3 * l + 2)
                norm(3 * l + 3, T_ffn, True, 3 * l + 3 < SUBS, AT["w13", 3 * l + 3] if 3 * l + 3 < SUBS else END)

        @block.tensor
        def _(pe):
            T = nc.tensor

            def three(out, a, b, start, stop):
                T.matmul(out, a[0], b[0], start=start, stop=False)
                T.matmul(out, a[0], b[1], start=False, stop=False)
                return T.matmul(out, a[1], b[0], start=False, stop=stop)

            def ready(u, k=0, step=0):
                pe.wait_ge(w_split, k * step + (u + 1))

            def form_a(u, bank, src, n, k=0, step=0, kts=KD, row=0, last=True, n0=0):
                s = u % RING
                if row == 0:
                    ready(u, k, step)
                for kt in range(kts):
                    c = (row + kt) * P
                    ins = three(ps[:, bank, n0:n], (wh[:, s, c:c + P], wl[:, s, c:c + P]),
                                (src[0][:, kt, n0:n], src[1][:, kt, n0:n]), kt == 0, kt == kts - 1)
                if last:
                    ins.then_inc(unit_done, 1)

            def ada(u, j, group, k=0, step=0):
                s = u % RING
                ready(u, k, step)
                if j == 0:
                    pe.wait_ge(ada_sum, (k if step else 0) + (group + 1))
                for a in range(2):
                    kt = 2 * j + a
                    T.matmul(ps[0:4, 4, :], cs[:, kt, :], wh[:, s, a * 512:(a + 1) * 512], start=kt == 0, stop=False)
                    ins = T.matmul(ps[0:4, 4, :], cs[:, kt, :], wl[:, s, a * 512:(a + 1) * 512], start=False, stop=kt == KD - 1)
                ins.then_inc(unit_done, 1)

            def gates(i, s):
                pe.wait_ge(mod_taken, i + 1)
                for a in range(2):
                    ins = T.matmul(ps[:, 6 - 2 * s + a, :], selb[32:36, s, :], mod4[32:36, a * 512:(a + 1) * 512],
                                   start=True, stop=True)
                ins.then_inc(gate_mm, 1)

            def modulations(i):
                pe.wait_ge(ada_sum, 1 + ADA_G * (i + 1))
                if i:
                    pe.wait_ge(post_stat, post0(i - 1) + 2)
                for k in range(2 * KD):
                    ins = T.transpose(ps[:, mod_bank(i), 4 * k:4 * k + 4], mod4[0:4, k * P:(k + 1) * P], ident[0:4, 0:4])
                ins.then_inc(mods_mm, 1)

            def turn(i, t):
                tB = (T_mix if i % 3 == 2 else T_ffn)[4]
                pe.wait_ge(pre_norm, pre0(i) + t + 1)
                for k in range(KD):
                    ins = T.transpose(ps[:, 2 * t + k // 4, (k % 4) * P:(k % 4 + 1) * P], tB[:, t, k * P:(k + 1) * P], ident[:])
                ins.then_inc(h_turned, 1)

            def begin(i, units):
                if i:
                    turn(i, 0)
                    modulations(i)
                    pe.wait_ge(mods_ready, i + 1)
                    turn(i, 1)
                pe.wait_ge(h_lo, pre0(i) + LT)
                if htiles(i) == LT:
                    for u, bank in units:
                        form_a(u, bank, (hh, hl), SEQ)
                    return
                for u, bank in units:
                    form_a(u, bank, (hh, hl), SEQ, last=False)
                if i:
                    turn(i, 2)
                    turn(i, 3)
                pe.wait_ge(h_lo, pre0(i + 1))
                for u, bank in units:
                    form_a(u, bank, (hh, hl), TOK, n0=SEQ)

            def form_b(i, u, n, made, count):
                b = stage0(i)

                def product(k0, t, first=False, last=False):
                    s = (u + k0) % RING
                    a = (sh_[:, k0 % TAIL, t * P:(t + 1) * P], sl_[:, k0 % TAIL, t * P:(t + 1) * P])
                    for h in range(2):
                        w = slice(h * 512, (h + 1) * 512)
                        ins = three(ps[:, 2 * t + h, :], a, (wh[:, s, w], wl[:, s, w]), first, last)
                    return ins

                def staged(k0, k=0):
                    pe.wait_ge(w_split, k * 4 + (u + k0 + 1))
                    pe.wait_ge(stage_lo, k * 4 + (b + k0 + 1))

                def step(k0, k=0):
                    staged(k0, k)
                    for t in range(tiles(i)):
                        ins = product(k0, t)
                    ins.then_inc(unit_done, 1)

                staged(0)
                late = (0, 1) if i % 3 != 1 else (2, 3)
                for t in [t for t in range(tiles(i)) if t not in late] + [t for t in range(tiles(i)) if t in late]:
                    if t == late[0]:
                        pe.wait_ge(made, count)
                    ins = product(0, t, first=True)
                ins.then_inc(unit_done, 1)
                body = n - TAIL - 1
                for k0 in range(1, 1 + body % 4):
                    step(k0)
                head = 1 + body % 4
                if body >= 4:
                    with loop(pe, body // 4) as k:
                        for j in range(4):
                            step(head + j, k)
                for t in range(tiles(i)):
                    for k0 in range(n - TAIL, n):
                        if t == 0:
                            staged(k0)
                        ins = product(k0, t, last=k0 == n - 1)
                        if t == tiles(i) - 1:
                            ins.then_inc(unit_done, 1)
                        elif k0 == n - 1:
                            ins.then_inc(y_tile, 1)

            def ffn(i):
                N, u, m = htiles(i) * P, AT["w13", i], ff0(i)
                src = (hh, hl)

                def pair(v, mt, j, k, step):
                    pe.wait_ge(ff_mul, k * 2 + (mt + 1))
                    form_a(v, 2 * j, src, N, k, step)
                    form_a(v + 1, 2 * j + 1, src, N, k, step)

                it0 = 0
                if i + 1 < SUBS:
                    def modulated(k0, k=0, step=0, fresh=True):
                        v = u + 8 * k0
                        for j in range(2):
                            if j or fresh:
                                pair(v + 4 * j, m + 2 * k0 + j, j, k, step)
                            for o in range(2):
                                ada(v + 4 * j + 2 + o, 2 * j + o, ADA_G * (i + 1) + k0, k, step)

                    begin(i, ((u, 0), (u + 1, 1)))
                    modulated(0, fresh=False)
                    with loop(pe, ADA_IT - 1) as k:
                        modulated(1, k, 8)
                    u += 8 * ADA_IT
                    it0 = ADA_IT
                else:
                    begin(i, ())
                for s in range(streams(i)):
                    if s:
                        pe.wait_ge(ada_sum, 1 + ADA_G * (i + 2))
                    gates(i, s)
                with loop(pe, FFN_IT - it0) as k:
                    for j in range(2):
                        pair(u + 2 * j, m + 2 * it0 + j, j, k, 4)
                pe.wait_ge(gate_ready, gate0(i + 1))
                form_b(i, AT["w2", i], KF, ff_mul, 2 + m + KF)

            def token_form(u, n, width_, tile_done):
                kt_per = UN // width_

                def product(k, t):
                    s = (u + k) % RING
                    for kk in range(kt_per):
                        kt = k * kt_per + kk
                        a = (hh[:, kt, t * P:(t + 1) * P], hl[:, kt, t * P:(t + 1) * P])
                        for h in range(width_ // 512):
                            w = slice(kk * 512 + h * 512, kk * 512 + (h + 1) * 512)
                            ins = three(ps[:, t * (width_ // 512) + h, :], a, (wh[:, s, w], wl[:, s, w]),
                                        kt == 0, kt == KD - 1)
                    return ins

                for k in range(n - TAIL):
                    ready(u + k)
                    for t in range(NT):
                        ins = product(k, t)
                    ins.then_inc(unit_done, 1)
                for t in range(NT):
                    for k in range(n - TAIL, n):
                        if t == 0:
                            ready(u + k)
                        ins = product(k, t)
                        if t == NT - 1:
                            ins.then_inc(unit_done, 1)
                        elif k == n - 1:
                            ins.then_inc(tile_done, 1)

            def retention(l):
                items, b = r_items[l], r0[l]

                def scores(t):
                    h, s = items[t]
                    if t >= 2:
                        pe.wait_ge(r_prob, b + t - 1)
                    for j, kt in enumerate(range(NT) if s == 0 else range(LT, NT)):
                        ins = T.matmul(ps[:, 2 * (t % 2) + j // 2, (j % 2) * SEQ:(j % 2 + 1) * SEQ],
                                       kq[:, h, kt * P:(kt + 1) * P], kq[:, 4 + h, s * SEQ:(s + 1) * SEQ],
                                       start=True, stop=True)
                    ins.then_inc(r_score, 1)

                def values(t):
                    h, s = items[t]
                    pe.wait_ge(r_prob, b + t + 1)
                    if t >= 3:
                        pe.wait_ge(r_used, b + t - 2)
                    kts = list(range(NT) if s == 0 else range(LT, NT))
                    for a in range(2):
                        for j, kt in enumerate(kts):
                            c = h * DV + a * P
                            ins = T.matmul(ps[:, 4 + t % 3, a * SEQ:(a + 1) * SEQ], rv[:, kt, c:c + P], rp[:, t % 2, j],
                                           start=j == 0, stop=j == len(kts) - 1)
                    ins.then_inc(r_out, 1)

                def variance(t):
                    pe.wait_ge(r_sq, b + t + 1)
                    if t >= 1:
                        pe.wait_ge(r_taken, b + t)
                    for q in range(LT):
                        for a in range(2):
                            ins = T.matmul(ps[:, 7, SEQ + q:SEQ + q + 1], rq2[:, a, q * P:(q + 1) * P], mean256[:, 0:1],
                                           start=a == 0, stop=a == 1)
                    ins.then_inc(r_var, 1)

                def spread(t):
                    pe.wait_ge(r_diag, b + t + 1)
                    T.matmul(ps[:, 7, 0:SEQ], mean256[:], rr[:, t % 2].rearrange("p q n -> p (q n)"), start=True, stop=True)\
                     .then_inc(r_spread, 1)

                pe.wait_ge(rv_copied, NT * l + 1)
                scores(0)
                pe.wait_ge(rv_copied, NT * (l + 1))
                for t in range(len(items) + 2):
                    if t < len(items):
                        values(t)
                    if t >= 2:
                        spread(t - 2)
                    if t + 1 < len(items):
                        scores(t + 1)
                    if 1 <= t <= len(items):
                        variance(t - 1)
                    if t == len(items):
                        pe.wait_ge(r_prob, b + t)
                        pe.wait_ge(in_copied, IN_A * l + 1 + 16)
                        form_a(AT["fu", l], 0, (hh, hl), mid(l))

            def attention(l):
                items, b = n_items[l], n0[l]
                per = len(items) // NH

                def scores(t):
                    h, s, q = items[t]
                    if t >= 3:
                        pe.wait_ge(n_exp, b + t - 2)
                    p0 = DH * (h % 2)
                    c = s * SEQ + q * P
                    T.matmul(ps[:, SCORE_BANKS[t % 3], 0:key_n(items[t])], nkq[p0:p0 + DH, 1, h // 2, c:c + P],
                             nkq[p0:p0 + DH, 0, h // 2, s * SEQ:TOK], start=True, stop=True).then_inc(n_score, 1)

                def turned(t):
                    pe.wait_ge(n_jd, b + t + 1)
                    if t >= 2:
                        pe.wait_ge(n_turnc, b + t - 1)
                    for j in range(key_n(items[t]) // P):
                        w = slice(j * P, (j + 1) * P)
                        ins = T.matmul(ps[:, 2 + t % 2, w], prob[:, t % 3, w], jd[:, t % 3], start=True, stop=True)
                    ins.then_inc(n_turn, 1)

                def values(t):
                    h, s, q = items[t]
                    pr = h // 2
                    pe.wait_ge(n_turnc, b + t + 1)
                    if t % (2 * per) == 0 and pr >= 2:
                        pe.wait_ge(n_lo, 4 * l + pr - 1)
                    p0, c = DH * (h % 2), s * SEQ + q * P
                    kts = list(range(NT) if s == 0 else range(LT, NT))
                    for j, kt in enumerate(kts):
                        ins = T.matmul(ps[p0:p0 + DH, 4 + pr % 2, c:c + P], nv[:, kt, h * DH:(h + 1) * DH],
                                       probT[:, t % 2, j * P:(j + 1) * P], start=j == 0, stop=j == len(kts) - 1)
                    ins.then_inc(n_out, 1)

                for t in range(len(items) + 3):
                    if t < len(items):
                        scores(t)
                    if 2 <= t < len(items) + 2:
                        turned(t - 2)
                    if t >= 3:
                        values(t - 3)

            def mixer(l):
                i, N, src = 3 * l + 1, mid(l), (hh, hl)
                G0 = ADA_G * (i + 1)
                c0 = IN_A * l + 1

                def inputs(u, idx, n, gi, fresh=True):
                    for j in range(4):
                        if j or fresh:
                            pe.wait_ge(in_copied, c0 + idx + j)
                            form_a(u + 2 * j, j, src, n)
                        ada(u + 2 * j + 1, j, G0 + gi)
                        if KD < idx + j < 2 * KD:
                            rope(idx + j - KD - 1)

                def rope(k):
                    pe.wait_ge(in_copied, c0 + 3 + KD + k + 1)
                    if k >= 2:
                        pe.wait_ge(rope_done, 8 * l + k - 1)
                    T.matmul(ps[:, 5 + k % 2, 0:SEQ], swap[:], kq[:, k, 0:SEQ], start=True, stop=True).then_inc(rope_mm, 1)

                u = AT["ret_in", l]
                if N == TOK:
                    begin(i, ((u, 0),))
                    inputs(u, 0, N, 0, fresh=False)
                else:
                    begin(i, ())
                    inputs(u, 0, N, 0)
                inputs(u + 8, 4, N, 1)
                inputs(u + 16, 8, TOK, 2)
                inputs(u + 24, 12, N, 3)
                rope(7)
                pe.wait_ge(in_copied, c0 + 3 + 16)
                pe.wait_ge(ada_sum, 1 + G0 + 4)
                pe.wait_ge(rope_done, 8 * (l + 1))
                token_form(AT["rv", l], KD, D, rv_tile)
                retention(l)
                for j in range(1, 4):
                    pe.wait_ge(in_copied, c0 + 16 + j)
                    form_a(AT["fu", l] + j, j, src, N)
                pe.wait_ge(in_copied, c0 + 3 + 20)
                pe.wait_ge(r_fin, r0[l] + len(r_items[l]))
                for t in range(len(f_items[l]) + 1):
                    if t < len(f_items[l]):
                        gr, s = f_items[l][t]
                        if t >= 2:
                            pe.wait_ge(f_onec, f0[l] + t - 1)
                        for a in range(2):
                            c = s * SEQ + a * P
                            ins = T.matmul(ps[:, 4 + t % 2, a * SEQ:(a + 1) * SEQ], fu[:, gr, c:c + P], dft_d[:], start=True, stop=True)
                        ins.then_inc(f_one, 1)
                    if t >= 1:
                        v = t - 1
                        pe.wait_ge(f_onec, f0[l] + v + 1)
                        if v >= 2:
                            pe.wait_ge(f_lo, f0[l] + v - 1)
                        for a in range(2):
                            for part in range(2):
                                ins = T.matmul(ps[:, 6 + v % 2, 0:SEQ], fA[:, v % 2, a, part * P:(part + 1) * P],
                                               dft_n[:, a, part, :], start=a + part == 0, stop=a + part == 2)
                        ins.then_inc(f_two, 1)
                u = AT["na_in", l]
                inputs(u, 20, TOK, 4)
                inputs(u + 8, 24, N, 5)
                pe.wait_ge(in_copied, c0 + 3 + IN_A)
                token_form(AT["nv", l], 4, 512, nv_tile)
                pe.wait_ge(nv_copied, NT * (l + 1))
                pe.wait_ge(ada_sum, 1 + G0 + 6)
                pe.wait_ge(f_lo, f0[l] + len(f_items[l]))
                attention(l)
                u = AT["merge", l]
                with loop(pe, 2) as k:
                    for mm in range(4):
                        v, sgn, smn = u + 5 * mm, 24 * l + 3 * mm, 40 * l + 5 * mm
                        pe.wait_ge(g_sig, k * 12 + (sgn + 1))
                        form_a(v, 0, src, N, k, 20)
                        pe.wait_ge(g_sum, k * 20 + (smn + 1))
                        if mm == 0:
                            pe.wait_ge(o_lo, 2 * (l + 1))
                        form_a(v + 1, 1, (oh, ol), N, k, 20)
                        pe.wait_ge(g_sig, k * 12 + (sgn + 2))
                        form_a(v + 2, 2, src, N, k, 20)
                        pe.wait_ge(g_sum, k * 20 + (smn + 4))
                        if mm == 0:
                            pe.wait_ge(n_lo, 4 * (l + 1))
                        form_a(v + 3, 3, (ah, al), N, k, 20, kts=4, last=False)
                        form_a(v + 3, 4, (fh, fl), N, k, 20, kts=4, row=4)
                        pe.wait_ge(g_sig, k * 12 + (sgn + 3))
                        form_a(v + 4, 5, src, N, k, 20)
                pe.wait_ge(g_sum, 5 + 40 * (l + 1))
                gates(i, 0)
                if streams(i) > 1:
                    gates(i, 1)
                form_b(i, AT["wo", l], KD, gate_ready, gate0(i + 1))

            pe.wait_ge(c_lo, 2)
            with loop(pe, ADA_G) as k:
                for j in range(ADA_U):
                    ada(j, j, 0, k, ADA_U)
            pe.wait_ge(ident_in, 16 * 2)
            turn(0, 0)
            turn(0, 1)
            modulations(0)
            pe.wait_ge(mods_ready, 1)
            turn(0, 2)
            turn(0, 3)
            for l in range(DEPTH):
                ffn(3 * l)
                mixer(l)
                ffn(3 * l + 2)


def constants():
    import numpy as np
    f32 = np.float32
    k = {"k_ident": np.eye(P, dtype=f32)}
    flip = np.zeros((P, P), f32)
    for r in range(P // GRID_W):
        for c in range(GRID_W):
            flip[r * GRID_W + GRID_W - 1 - c, r * GRID_W + c] = 1
    k["k_flip"] = flip
    swap = np.zeros((P, P), f32)
    C, S = np.zeros((P, SEQ), f32), np.zeros((P, SEQ), f32)
    pos = np.arange(SEQ)
    q = DK // 4
    freq = (f32(10000.0) ** (-np.arange(q, dtype=f32) / f32(q))).astype(f32)
    for half, p in enumerate((pos // GRID_W, pos % GRID_W)):
        ang = p.astype(f32)[None, :] * freq[:, None]
        for a in range(2):
            rows = slice(half * 2 * q + a * q, half * 2 * q + (a + 1) * q)
            C[rows], S[rows] = np.cos(ang), np.sin(ang)
        for j in range(q):
            m = half * 2 * q + j
            swap[m + q, m] = -1
            swap[m, m + q] = 1
    k["k_swap"], k["k_rope_c"], k["k_rope_s"] = swap, C, S
    d = np.arange(P)
    ang = 2 * np.pi * (np.outer(d, d) % P) / P
    k["k_dft_d"] = np.concatenate([np.cos(ang), np.sin(ang)], 1).astype(f32)
    n = np.arange(SEQ)
    ang = 2 * np.pi * (np.outer(n, n) % SEQ) / SEQ
    s = 1 / np.sqrt(SEQ * P)
    both = np.stack([np.cos(ang) * s, -np.sin(ang) * s], 1).astype(f32)
    k["k_dft_n"] = np.ascontiguousarray(both.reshape(2, P, 2, SEQ).transpose(1, 0, 2, 3))
    cq = GRID_W - 1 - np.arange(P) % GRID_W
    start = np.clip(cq - 8, 0, GRID_W - 16)
    ck = np.arange(GRID_W)
    inside = (ck[None] >= start[:, None]) & (ck[None] < start[:, None] + 16)
    k["k_wmask"] = np.where(inside, 0, -1e30).astype(f32)
    sel = np.array([[1, 0], [1, 0], [0, 1], [0, 1]], f32)
    k["k_selb"] = np.ascontiguousarray(np.broadcast_to(sel[:, :, None], (4, 2, P)))
    k["k_zero"] = np.zeros((1, 3 * D), f32)
    key = (np.arange(2)[None, :, None] * P + np.arange(P)[:, None, None]).astype(f32)
    qry = np.arange(SEQ, dtype=f32)[None, None, :]
    k["k_dist"] = np.ascontiguousarray(np.stack([np.maximum(qry - key, 0), np.maximum(key - qry, 0),
                                                 qry + CTX - key, SEQ - qry + key], 1).astype(f32))
    return k


_INS = ['x', 'c', 'ctx', 'c_ctx', 'ada_w', 'ada_b', 'ln_w', 'ln_b', 'ffa_w1', 'ffa_w3', 'ffa_w2', 'mix_w_in',
        'ret_decay_logit', 'ret_gn_w', 'ret_gn_b', 'ret_w_out', 'na_rpb', 'mix_w_o',
        'ffb_w1', 'ffb_w3', 'ffb_w2']


def kernel(**inputs):
    import numpy as np
    import concourse.bacc as bacc
    from concourse.bass_utils import run_bass_kernel_spmd

    nc = bacc.Bacc("TRN2", target_bir_lowering=False, num_devices=1, dynamic_dma_scratch_size=512)
    arrays, io = {}, {}
    both = [("na_fou_w_out", np.concatenate([inputs["na_w_out"], inputs["fou_w_out"]], axis=1))]
    for name, a in [(n, inputs[n]) for n in _INS] + both + list(constants().items()):
        a = np.ascontiguousarray(a)
        arrays[f"in_{name}"] = a
        io[name] = nc.dram_tensor(f"in_{name}", a.shape, mybir.dt.from_np(a.dtype), kind="ExternalInput").ap()
    out = nc.dram_tensor("out_0", (1, SEQ, D), F32, kind="ExternalOutput").ap()
    trunk(nc, io, out)
    r = run_bass_kernel_spmd(nc, [arrays], core_ids=[0])
    return r.results[0]["out_0"]
```
